# Optimizing a Trainium2 kernel written in Bass

```python
import math
import jax, jax.numpy as jnp
from jax import lax
import numpy as np

D_MODEL = 2048
BATCH = 1
SEQ = 256
DEPTH = 1

D_INNER_A = 3 * D_MODEL // 2
HEAD_DIM_A = 64
N_HEADS_A = D_INNER_A // HEAD_DIM_A
N_GROUPS_A = 8
HEADS_PER_GROUP = N_HEADS_A // N_GROUPS_A
D_STATE_A = 128
CONV_A = 4
CHUNK = 256
CONV_DIM_A = D_INNER_A + 2 * N_GROUPS_A * D_STATE_A
D_S5 = D_MODEL // 2
S5_GROUP = 16
N_GROUPS_S5 = D_S5 // S5_GROUP
S5_STATE = 64
D_FF = 256 * ((8 * D_MODEL // 3 + 255) // 256)
CONV_FFN = 3
EPS = 1e-6
DT_MIN = 1e-3
DT_MAX = 1e-1
EIG_MAX = -1e-4
IN_COLS = D_INNER_A + CONV_DIM_A + N_HEADS_A + D_S5 + 2 * D_MODEL

kernel_name = "hybrid_ssd_s5_gated_convffn"

def rmsnorm(x, w):
    xf = x.astype(jnp.float32)
    xf = xf * lax.rsqrt(jnp.mean(xf * xf, axis=-1, keepdims=True) + EPS)
    return xf.astype(x.dtype) * w

def causal_dwconv(x, w, b):
    k = w.shape[0]
    y = lax.conv_general_dilated(
        x, w[:, None, :].astype(x.dtype), window_strides=(1,), padding=[(k - 1, 0)],
        dimension_numbers=("NWC", "WIO", "NWC"), feature_group_count=x.shape[-1])
    return y + b

def segsum(a):
    t = a.shape[-1]
    ar = jnp.broadcast_to(a[..., :, None], a.shape + (t,))
    strict = jnp.tril(jnp.ones((t, t), dtype=bool), k=-1)
    cs = jnp.cumsum(jnp.where(strict, ar, 0.0), axis=-2)
    incl = jnp.tril(jnp.ones((t, t), dtype=bool), k=0)
    return jnp.where(incl, cs, -jnp.inf)

def ssd_chunked(xh, da, bm, cm):
    b, seqlen = xh.shape[:2]
    nc = -(-seqlen // CHUNK)
    pad = nc * CHUNK - seqlen
    if pad:
        xh = jnp.pad(xh, ((0, 0), (0, pad), (0, 0), (0, 0), (0, 0)))
        da = jnp.pad(da, ((0, 0), (0, pad), (0, 0), (0, 0)))
        bm = jnp.pad(bm, ((0, 0), (0, pad), (0, 0), (0, 0)))
        cm = jnp.pad(cm, ((0, 0), (0, pad), (0, 0), (0, 0)))
    X = xh.reshape(b, nc, CHUNK, N_GROUPS_A, HEADS_PER_GROUP, HEAD_DIM_A)
    A = da.reshape(b, nc, CHUNK, N_GROUPS_A, HEADS_PER_GROUP).transpose(0, 3, 4, 1, 2)
    Bc = bm.reshape(b, nc, CHUNK, N_GROUPS_A, D_STATE_A)
    Cc = cm.reshape(b, nc, CHUNK, N_GROUPS_A, D_STATE_A)
    a_cs = jnp.cumsum(A, axis=-1)
    decay_in = jnp.exp(segsum(A))
    cb = jnp.einsum("bclgn,bcsgn->bgcls", Cc, Bc)
    y_diag = jnp.einsum("bgcls,bgrcls,bcsgrp->bclgrp", cb, decay_in, X)
    decay_states = jnp.exp(a_cs[..., -1:] - a_cs)
    states = jnp.einsum("bclgn,bgrcl,bclgrp->bcgrpn", Bc, decay_states, X)
    states = jnp.concatenate([jnp.zeros_like(states[:, :1]), states], axis=1)
    chunk_decay = jnp.exp(segsum(jnp.pad(a_cs[..., -1], ((0, 0), (0, 0), (0, 0), (1, 0)))))
    new_states = jnp.einsum("bgrzc,bcgrpn->bzgrpn", chunk_decay, states)
    states = new_states[:, :-1]
    y_off = jnp.einsum("bclgn,bcgrpn,bgrcl->bclgrp", Cc, states, jnp.exp(a_cs))
    y = (y_diag + y_off).reshape(b, nc * CHUNK, N_GROUPS_A, HEADS_PER_GROUP, HEAD_DIM_A)
    return y[:, :seqlen]

def mamba2_mixer(z, xbc, dt_raw, conv_w, conv_b, dt_bias, a_log, d_skip, norm_w, w_proj):
    b, seqlen, _ = z.shape
    f32 = jnp.float32
    xbc = jax.nn.silu(causal_dwconv(xbc, conv_w, conv_b))
    gn = N_GROUPS_A * D_STATE_A
    xs, bm, cm = jnp.split(xbc, [D_INNER_A, D_INNER_A + gn], axis=-1)
    dt = jax.nn.softplus(dt_raw.astype(f32) + dt_bias.astype(f32))
    a = -jnp.exp(a_log.astype(f32))
    dt_g = dt.reshape(b, seqlen, N_GROUPS_A, HEADS_PER_GROUP)
    xh = xs.astype(f32).reshape(b, seqlen, N_GROUPS_A, HEADS_PER_GROUP, HEAD_DIM_A)
    y = ssd_chunked(xh * dt_g[..., None],
                    dt_g * a.reshape(N_GROUPS_A, HEADS_PER_GROUP),
                    bm.astype(f32).reshape(b, seqlen, N_GROUPS_A, D_STATE_A),
                    cm.astype(f32).reshape(b, seqlen, N_GROUPS_A, D_STATE_A))
    y = y + d_skip.astype(f32).reshape(N_GROUPS_A, HEADS_PER_GROUP)[:, :, None] * xh
    y = y.reshape(b, seqlen, D_INNER_A) * jax.nn.silu(z.astype(f32))
    yg = y.reshape(b, seqlen, N_GROUPS_A, D_INNER_A // N_GROUPS_A)
    yg = yg * lax.rsqrt(jnp.mean(yg * yg, axis=-1, keepdims=True) + EPS)
    y = yg.reshape(b, seqlen, D_INNER_A).astype(z.dtype) * norm_w
    return y @ w_proj

def _lin_rec(e1, e2):
    a1, b1 = e1
    a2, b2 = e2
    return a1 * a2, a2 * b1 + b2

def s5_mixer(u, lam_re, lam_im, log_dt, b_re, b_im, c_re, c_im, d_skip, w_glu):
    b, seqlen, _ = u.shape
    f32 = jnp.float32
    ug = u.astype(f32).reshape(b, seqlen, N_GROUPS_S5, S5_GROUP)
    lam = lax.complex(jnp.minimum(lam_re.astype(f32), EIG_MAX), lam_im.astype(f32))
    dt = jnp.exp(log_dt.astype(f32))[:, None]
    lam_bar = jnp.exp(lam * dt)
    bmat = lax.complex(b_re.astype(f32), b_im.astype(f32))
    cmat = lax.complex(c_re.astype(f32), c_im.astype(f32))
    b_bar = ((lam_bar - 1.0) / lam)[..., None] * bmat
    bu = jnp.einsum("gpc,blgc->blgp", b_bar, ug.astype(jnp.complex64))
    a_el = jnp.broadcast_to(lam_bar, bu.shape)
    _, states = lax.associative_scan(_lin_rec, (a_el, bu), axis=1)
    y = jnp.einsum("gcp,blgp->blgc", cmat, states).real + d_skip.astype(f32).reshape(N_GROUPS_S5, S5_GROUP) * ug
    y = jax.nn.gelu(y.reshape(b, seqlen, D_S5)).astype(u.dtype)
    val, gate = jnp.split(y @ w_glu, 2, axis=-1)
    return val * jax.nn.sigmoid(gate)

def conv_glu_ffn(hn, w_up, conv_w, conv_b, w_down):
    up = causal_dwconv(hn @ w_up, conv_w, conv_b)
    gate, val = jnp.split(up, 2, axis=-1)
    return (jax.nn.silu(gate) * val) @ w_down

def setup_inputs(seed: int = 0) -> dict:
    key = jax.random.key(seed)
    ks = jax.random.split(key, 28)
    f32 = jnp.float32
    L = DEPTH

    def nrm(k, shape, scale):
        return jax.random.normal(k, shape, f32) * scale

    log_lo, log_hi = math.log(DT_MIN), math.log(DT_MAX)
    dt0 = jnp.exp(jax.random.uniform(ks[6], (L, N_HEADS_A), f32, log_lo, log_hi))
    dt_bias = dt0 + jnp.log(-jnp.expm1(-dt0))
    lam_im0 = math.pi * jnp.arange(S5_STATE, dtype=f32)
    return {
        "x": nrm(ks[0], (BATCH, SEQ, D_MODEL), 1.0),
        "norm_mix_w": 1.0 + nrm(ks[1], (L, D_MODEL), 0.02),
        "w_in": nrm(ks[2], (L, D_MODEL, IN_COLS), D_MODEL ** -0.5),
        "conv_a_w": nrm(ks[3], (L, CONV_A, CONV_DIM_A), CONV_A ** -0.5),
        "conv_a_b": nrm(ks[4], (L, CONV_DIM_A), 0.01),
        "dt_bias": dt_bias,
        "a_log": jnp.log(jax.random.uniform(ks[7], (L, N_HEADS_A), f32, 1.0, 16.0)),
        "d_a": 1.0 + nrm(ks[8], (L, N_HEADS_A), 0.02),
        "norm_a_w": 1.0 + nrm(ks[9], (L, D_INNER_A), 0.02),
        "w_proj_a": nrm(ks[10], (L, D_INNER_A, D_MODEL), D_INNER_A ** -0.5),
        "s5_lam_re": -0.5 + nrm(ks[11], (L, N_GROUPS_S5, S5_STATE), 0.01),
        "s5_lam_im": lam_im0 + nrm(ks[12], (L, N_GROUPS_S5, S5_STATE), 0.01),
        "s5_log_dt": jax.random.uniform(ks[13], (L, N_GROUPS_S5), f32, log_lo, log_hi),
        "s5_b_re": nrm(ks[14], (L, N_GROUPS_S5, S5_STATE, S5_GROUP), (2 * S5_GROUP) ** -0.5),
        "s5_b_im": nrm(ks[15], (L, N_GROUPS_S5, S5_STATE, S5_GROUP), (2 * S5_GROUP) ** -0.5),
        "s5_c_re": nrm(ks[16], (L, N_GROUPS_S5, S5_GROUP, S5_STATE), S5_STATE ** -0.5),
        "s5_c_im": nrm(ks[17], (L, N_GROUPS_S5, S5_GROUP, S5_STATE), S5_STATE ** -0.5),
        "s5_d": nrm(ks[18], (L, D_S5), 1.0),
        "w_s5_glu": nrm(ks[19], (L, D_S5, 2 * D_MODEL), D_S5 ** -0.5),
        "w_out": nrm(ks[20], (L, D_MODEL, D_MODEL), D_MODEL ** -0.5),
        "norm_ffn_w": 1.0 + nrm(ks[21], (L, D_MODEL), 0.02),
        "w_up": nrm(ks[22], (L, D_MODEL, 2 * D_FF), D_MODEL ** -0.5),
        "conv_ffn_w": nrm(ks[23], (L, CONV_FFN, 2 * D_FF), CONV_FFN ** -0.5),
        "conv_ffn_b": nrm(ks[24], (L, 2 * D_FF), 0.01),
        "w_down": nrm(ks[25], (L, D_FF, D_MODEL), D_FF ** -0.5),
        "norm_final_w": 1.0 + nrm(ks[26], (D_MODEL,), 0.02),
    }

def reference(x, norm_mix_w, w_in, conv_a_w, conv_a_b, dt_bias, a_log, d_a, norm_a_w, w_proj_a,
              s5_lam_re, s5_lam_im, s5_log_dt, s5_b_re, s5_b_im, s5_c_re, s5_c_im, s5_d, w_s5_glu,
              w_out, norm_ffn_w, w_up, conv_ffn_w, conv_ffn_b, w_down, norm_final_w):
    sizes = [D_INNER_A, CONV_DIM_A, N_HEADS_A, D_S5, D_MODEL, D_MODEL]
    splits = [int(s) for s in np.cumsum(sizes)[:-1]]
    h = x
    for i in range(DEPTH):
        hn = rmsnorm(h, norm_mix_w[i])
        z, xbc, dt_raw, u, g_a, g_b = jnp.split(hn @ w_in[i], splits, axis=-1)
        y_a = mamba2_mixer(z, xbc, dt_raw, conv_a_w[i], conv_a_b[i], dt_bias[i], a_log[i], d_a[i],
                           norm_a_w[i], w_proj_a[i])
        y_b = s5_mixer(u, s5_lam_re[i], s5_lam_im[i], s5_log_dt[i], s5_b_re[i], s5_b_im[i],
                       s5_c_re[i], s5_c_im[i], s5_d[i], w_s5_glu[i])
        merged = jax.nn.sigmoid(g_a) * y_a + jax.nn.sigmoid(g_b) * y_b
        h = h + merged @ w_out[i]
        hn = rmsnorm(h, norm_ffn_w[i])
        h = h + conv_glu_ffn(hn, w_up[i], conv_ffn_w[i], conv_ffn_b[i], w_down[i])
    return rmsnorm(h, norm_final_w)


_drawn_inputs = setup_inputs


def setup_inputs(seed=0):
    import zlib

    import numpy as np

    out = dict(_drawn_inputs(seed))
    spreads = {}
    factors = {'norm_mix_w': 3.215,
     'conv_a_b': 7.714,
     'd_a': 64.0,
     'norm_a_w': 5.297,
     's5_lam_re': 64.0,
     's5_lam_im': 28.192,
     's5_log_dt': 29.088,
     's5_b_re': 39.352,
     's5_b_im': 39.904,
     's5_c_re': 40.024,
     's5_c_im': 39.776,
     'norm_ffn_w': 4.092,
     'conv_ffn_b': 8.0,
     'norm_final_w': 8.395}
    for name, (base, spread) in spreads.items():
        noise = np.random.default_rng([zlib.crc32(name.encode()), seed]).standard_normal(out[name].shape)
        drawn = base * np.exp(spread * noise) if base else spread * noise
        out[name] = __import__('jax').numpy.asarray(drawn.astype(out[name].dtype))
    for name, factor in factors.items():
        out[name] = (out[name] * factor).astype(out[name].dtype)
    return out
```

```python
import math
from contextlib import ExitStack

import numpy as np
import concourse.bass as bass
from concourse import mybir

F32, F32R, I32 = mybir.dt.float32, mybir.dt.float32r, mybir.dt.int32
ALU, ACTF = mybir.AluOpType, mybir.ActivationFunctionType
ds = bass.ds

P = 128
L = 256
D_MODEL, D_INNER, D_S5, D_FF = 2048, 3072, 1024, 5632
HEADS, GROUPS = 48, 8
HPG = HEADS // GROUPS
HALF = HPG // 2
TPG = D_INNER // GROUPS // P
EPS, EIG_MAX = 1e-6, -1e-4
KT = D_MODEL // P
S5T = 32
RING = 4
UNIT = 4 * 256
ML = L + P

PHASES = {"dt": (1, 4, 1), "u": (4, 4, 2), "z": (12, 4, 4), "x": (12, 4, 4), "bc": (8, 4, 4), "gate": (16, 4, 2),
          "proj": (8, 6, 2), "glu": (16, 2, 2), "out": (8, 4, 2), "up": (44, 4, 2), "down": (8, 11, 4)}
UNIT0, GROUP0, N_UNITS, N_ALL = {}, {}, 0, 0
for _n, (_g, _q, _b) in PHASES.items():
    UNIT0[_n], GROUP0[_n] = N_UNITS, N_ALL
    N_UNITS, N_ALL = N_UNITS + _g * _q, N_ALL + _g

PARM = {}
_at = 0
for _n, _w in (("norm_mix", 16), ("norm_ffn", 16), ("norm_final", 16), ("norm_a", 24), ("d_a", 24),
               ("conv_a_w", 160), ("conv_a_b", 40), ("conv_f_w", 264), ("conv_f_b", 88), ("s5_d", 8)):
    PARM[_n] = _at
    _at += _w
N_PARM = _at

LOG2E, LN2_HI, LN2_LO = 1.4426950408889634, 0.693359375, -2.12194440054690583e-4
MAGIC = 12582912.0
TWO_PI = 6.2831850


class Tally:

    def __init__(self, eng, sem):
        self.eng, self.sem, self.n, self.i, self.per, self.start = eng, sem, 0, None, 0, 0

    def enter(self, i, per):
        self.i, self.per, self.start = i, per, self.n

    def leave(self, turns):
        assert self.n - self.start == self.per, f"{self.n - self.start} steps in a turn, not {self.per}"
        self.i, self.n = None, self.start + turns * self.per

    def done(self, ins):
        ins.then_inc(self.sem, 1)
        self.n += 1
        self.eng.wait_ge(self.sem, self.n if self.i is None else self.i * self.per + self.n)


def build_program(nc, a, out):
    ctx = ExitStack()
    with ctx:
        base = nc.sbuf_base + -nc.sbuf_base % 64
        room = nc.sbuf_usable_end - base
        K = 1024

        def at(name, shape, dt, off):
            size = 4 * math.prod(shape[1:])
            assert off + size <= room, (name, off, size, room)
            return nc.alloc_sbuf_tensor_at(name, shape, dt, offset=base + off)

        raw = at("raw", [P, RING, UNIT], F32, 0)
        whi = at("whi", [P, RING, UNIT], F32R, 16 * K)
        wlo = at("wlo", [P, RING, UNIT], F32R, 32 * K)
        act16 = at("act16", [P, KT, 2 * L], F32R, 48 * K)
        zx = at("zx", [P, 24, 2, L], F32, 80 * K)
        y_hl = at("y_hl", [P, 24, 2 * L], F32R, 80 * K)
        vn = at("vn", [P, KT, L], F32, 80 * K)
        ff = at("ff", [P, 44, 2 * L], F32R, 80 * K)
        gates = at("gates", [P, 32, L], F32, 128 * K)
        bc = at("bc", [P, GROUPS, 2, L], F32, 152 * K)
        xin = at("xin", [P, KT, L], F32, 152 * K)
        ub = at("ub", [P, 8, L], F32, 168 * K)
        h = at("h", [P, KT, L], F32, 168 * K)
        yb_hl = at("yb_hl", [P, 8, 2 * L], F32R, 181 * K)
        tab = at("tab", [P, 2, L], F32, 128 * K)
        ang = at("ang", [P, 2, L], F32, 130 * K)
        rot1 = at("rot1", [P, 2, L], F32, 132 * K)
        rot2 = at("rot2", [P, 2, L], F32, 134 * K)
        st = at("st", [P, 2, L], F32, 136 * K)
        bz = at("bz", [P, 4, 2, P], F32, 138 * K)
        cz = at("cz", [P, 4, 2, 32], F32, 142 * K)
        cfold = at("cfold", [P, 2, S5T, 16], F32, 143 * K)
        iota = at("iota", [P, L], F32, 147 * K)
        s5in = at("s5in", [P, 3, S5T], F32, 148 * K)
        craw = at("craw", [P, 2, S5T, 16], F32, 96 * K)
        ctmp = at("ctmp", [P, 2, S5T, 16], F32, 100 * K)
        s5p = at("s5p", [P, 20, S5T], F32, 104 * K)
        s5i = at("s5i", [P, S5T], I32, 107 * K)
        iotai = at("iotai", [P, L], I32, 108 * K)
        xsq = at("xsq", [P, KT, L], F32, 112 * K)
        W = 176 * K
        dec = [at(f"dec{k}", [P, HALF, ML], F32, W + k * 4608) for k in range(2)]
        xst = at("xst", [P, TPG, L], F32, W + 9216)
        xtok = at("xtok", [P, 2, HPG * 64], F32, W + 12288)
        cbm = at("cbm", [P, ML], F32, W + 15360)
        mask = at("mask", [P, ML], F32, W + 16896)
        mask_in = at("mask_in", [P, ML], F32, W + 18432)
        ident = at("ident", [P, P], F32, W + 19968)
        dtt = at("dtt", [P, 2, HEADS], F32, W + 20480)
        dtw = at("dtw", [P, 7, L], F32, W)
        C = W + 21 * K
        hsum = at("hsum", [P, 2, L], F32, C)
        tsum = at("tsum", [P, 2, L], F32, C + 2048)
        bst = at("bst", [P, L], F32, C + 2048)
        cpad = at("cpad", [P, 2, L + 4], F32, C + 4096)
        parm = at("parm", [P, N_PARM], F32, C + 6208)
        rs = at("rs", [P, L], F32, C + 8832)
        sq = at("sq", [P, 2, L], F32, 185 * K)
        sqacc = at("sqacc", [P, 2, L], F32, 187 * K)
        ones = at("ones", [P, P], F32, C + 9856)
        s5k = at("s5k", [P, 2, S5T], F32, C + 10368)
        dtp = at("dtp", [P, 3], F32, C + 10624)
        scr = nc.dram_tensor("decay_rows", (HEADS, L), F32).ap()

        psum = ctx.enter_context(nc.psum_tensor("psum", [P, 8, 512], F32))
        BU, YS5 = psum[:, 4, :].rearrange("p (c n) -> p c n", c=2), psum[:, 5, 0:L]
        CB, XP = psum[:, 4, 0:ML], [psum[:, 5, 0:ML], psum[:, 6, 0:ML]]
        YY = [psum[:, 7, 0:L], psum[:, 7, L:2 * L], psum[:, 4, 0:L]]
        NS = psum[:, 6, 0:L]
        DTT = psum[:, 7, 0:2 * HEADS].rearrange("p (s h) -> p s h", s=2)

        def sem(name):
            return ctx.enter_context(nc.semaphore(name))

        x_in, w_in, b_in = [[sem(f"{n}{k}") for k in range(4)] for n in ("x_in", "w_in", "b_in")]
        parm_in, s5_in, h_in, out_done, scr_w = map(sem, ("parm_in", "s5_in", "h_in", "out_done", "scr_w"))
        dec_in = [sem("dec_in0"), sem("dec_in1")]
        hi_ready, lo_ready, unit_used, hsum_ready, sum_ready = map(
            sem, ("hi_ready", "lo_ready", "unit_used", "hsum_ready", "sum_ready"))
        dve_step, act_step, pool_step, const_ready = map(sem, ("dve_step", "act_step", "pool_step", "const_ready"))
        xsq_ready, sq_ready, sqacc_ready, ns_ready, rs_ready, v_ready, vhi_ready, vlo_ready = map(
            sem, ("xsq_ready", "sq_ready", "sqacc_ready", "ns_ready", "rs_ready", "v_ready", "vhi_ready", "vlo_ready"))
        dt_in, dt_exp, dt_row, dt_T, dt_v = map(sem, ("dt_in", "dt_exp", "dt_row", "dt_T", "dt_v"))
        th_ready, sincos, bu_ready, ang_ready, tab_ready, x5_ready, y5_ready, cz_ready, y5_out, y5_gelu, y5_hi, y5_lo = map(
            sem, ("th_ready", "sincos", "bu_ready", "ang_ready", "tab_ready", "x5_ready", "y5_ready", "cz_ready",
                  "y5_out", "y5_gelu", "y5_hi", "y5_lo"))
        z_done, conv_done, xbc_done, staged, cb_ready, xp_ready, scan_ready, exp_ready, m_ready, y_ready = map(
            sem, ("z_done", "conv_done", "xbc_done", "staged", "cb_ready", "xp_ready", "scan_ready", "exp_ready",
                  "m_ready", "y_ready"))
        yz_ready, ysq_ready, yns_ready, yrs_ready, yv_ready, yhi_ready, ylo_ready = map(
            sem, ("yz_ready", "ysq_ready", "yns_ready", "yrs_ready", "yv_ready", "yhi_ready", "ylo_ready"))
        ga_sig, gb_sig, glu_sig, m_sum, m_hi, m_lo, conv2_done, silu2_done, f_sum, f_hi, f_lo = map(
            sem, ("ga_sig", "gb_sig", "glu_sig", "m_sum", "m_hi", "m_lo", "conv2_done", "silu2_done", "f_sum",
                  "f_hi", "f_lo"))

        block = ctx.enter_context(nc.Block())

        def col(name, n):
            return parm[:, ds(n + PARM[name], 1)]

        def sums(g, half):
            b = 2 * (g % 2)
            return psum[:, b:b + 2, half * L:half * L + L]

        @block.sync
        def _(sp):
            for c in range(4):
                sp.dma_start(xin[:, 4 * c:4 * c + 4, :], a["x"][:, 4 * c:4 * c + 4, :]).then_inc(x_in[c], 16)
            for n in range(RING):
                sp.dma_start(raw[:, n, :], a["w_dt"][n]).then_inc(w_in[n], 16)
            sp.dma_start(parm[:, :], a["parm"]).then_inc(parm_in, 16)
            sp.dma_start(dtp[0:HEADS, 0:2], a["dtp"]).then_inc(parm_in, 16)
            sp.dma_start(s5in[:, :, :], a["s5_lam"]).then_inc(s5_in, 16)
            sp.dma_start(craw[:, :, :, :], a["s5_c"]).then_inc(s5_in, 16)
            for name in list(PHASES)[1:]:
                groups, quads, per = PHASES[name]
                if name == "out":
                    sp.wait_ge(unit_used, UNIT0["out"])
                    sp.dma_start(h[:, :, :], a["x"]).then_inc(h_in, 16)
                with sp.Fori(0, groups // per) as i:
                    for j in range(per * quads):
                        n = UNIT0[name] + j
                        sp.wait_ge(lo_ready, i * (per * quads) + (n - RING + 1))
                        sp.dma_start(raw[:, n % RING, :],
                                     a["w_" + name][ds(i * (per * quads) + j, 1), :, :]
                                     .rearrange("o p n -> (o p) n")).then_inc(w_in[n % RING], 16)
            for c in range(4):
                sp.wait_ge(v_ready, 8 + c + 1)
                sp.dma_start(out[:, 4 * c:4 * c + 4, :], vn[:, 4 * c:4 * c + 4, :]).then_inc(out_done, 16)
            sp.wait_ge(out_done, 64)

        @block.gpsimd
        def _(pool):
            step = Tally(pool, pool_step)
            nc.gpsimd.memset(ones[:, :], 1.0).then_inc(const_ready, 1)
            step.done(nc.gpsimd.memset(bz[:, :, :, :], 0.0))

            def load_b(blk, r):
                for g in range(2):
                    pool.dma_start(bz[32 * r + 16 * g:32 * r + 16 * g + 16, r, :, 64 * g:64 * g + 64],
                                   a["s5_b"][ds(blk * 8 + (2 * r + g), 1), :, :, :]
                                   .rearrange("o c k n -> (o c) k n")).then_inc(b_in[r], 16)

            def load_decay(g, half):
                rows = scr[ds(g * HPG + half * HALF, HALF), :]
                for lo, off in ((0, 0), (P, L)):
                    pool.dma_start(dec[half][:, :, off:off + L - lo],
                                   rows[:, lo:L].rearrange("(o h) n -> o h n", o=1).to_broadcast([P, HALF, L - lo])
                                   ).then_inc(dec_in[half], 16)

            for r in range(4):
                load_b(0, r)
            nc.gpsimd.memset(cz[:, :, :, :], 0.0).then_inc(const_ready, 1)
            nc.gpsimd.memset(cpad[:, :, :], 0.0).then_inc(const_ready, 1)
            nc.gpsimd.iota(iotai[:, :], pattern=[[1, L]], base=0, channel_multiplier=0).then_inc(const_ready, 1)
            step.done(nc.gpsimd.memset(ident[:, :], 0.0))
            nc.gpsimd.affine_select(out=ident[:, :], in_=ident[:, :], compare_op=ALU.not_equal, fill=1.0, base=0,
                                    pattern=[[-1, P]], channel_multiplier=1).then_inc(const_ready, 1)
            for m, keep in ((mask, ALU.is_gt), (mask_in, ALU.is_ge)):
                step.done(nc.gpsimd.memset(m[:, :], 1.0))
                for off, width in ((0, L), (L, P)):
                    nc.gpsimd.affine_select(out=m[:, off:off + width], in_=m[:, off:off + width], compare_op=keep,
                                            fill=0.0, base=0, pattern=[[1, width]],
                                            channel_multiplier=-1).then_inc(const_ready, 1)
            pool.wait_ge(dt_row, 1)
            pool.dma_start(scr[:, :], dtw[0:HEADS, 5, :]).then_inc(scr_w, 16)
            with pool.Fori(0, 7) as i:
                for r in range(4):
                    pool.wait_ge(bu_ready, i * 4 + (r + 1))
                    load_b(i + 1, r)
            pool.wait_ge(scr_w, 16)
            pool.wait_ge(dt_v, 1)
            for half in range(2):
                load_decay(0, half)
            with pool.Fori(0, GROUPS - 1) as i:
                for half in range(2):
                    pool.wait_ge(y_ready, i * 2 + (half + 1))
                    load_decay(i + 1, half)
            for n in range(2):
                pool.wait_ge(ns_ready, n + 1)
                pool.wait_ge(sum_ready, GROUP0["out" if n == 0 else "down"])
                nc.gpsimd.memset(sqacc[:, :, :], 0.0).then_inc(sqacc_ready, 1)
                with pool.Fori(0, 8) as i:
                    pool.wait_ge(sqacc_ready, i + (9 * n + 1))
                    pool.wait_ge(sq_ready, i + (8 * n + 1))
                    nc.gpsimd.tensor_tensor(sqacc[:, :, :], sqacc[:, :, :], sq[:, :, :],
                                            ALU.add).then_inc(sqacc_ready, 1)

        @block.scalar
        def _(act):
            step = Tally(act, act_step)
            fn = nc.scalar.activation

            def split_hi(n, ahead=0):
                s = n % RING
                act.wait_ge(w_in[s], ahead * (16 // RING) + 16 * (n // RING + 1))
                if n >= RING:
                    act.wait_ge(unit_used, ahead + (n - RING + 1))
                fn(whi[:, s, :], raw[:, s, :], ACTF.Copy).then_inc(hi_ready, 1)

            def take_hsum(g, end, gi=0, ui=0):
                act.wait_ge(unit_used, ui + end)
                if g:
                    act.wait_ge(sum_ready, gi + g)
                fn(hsum[:, :, :], sums(g, 1), ACTF.Copy).then_inc(hsum_ready, 1)

            def root(count, to):
                step.done(fn(rs[:, :], NS, ACTF.Ln, bias=EPS, scale=1.0 / count))
                fn(rs[:, :], rs[:, :], ACTF.Exp, scale=-0.5).then_inc(to, 1)

            def norm_hi(n):
                for c in range(4):
                    act.wait_ge(v_ready, 4 * n + c + 1)
                    fn(act16[:, 4 * c:4 * c + 4, 0:L], vn[:, 4 * c:4 * c + 4, :], ACTF.Copy).then_inc(vhi_ready, 1)

            def phase(name):
                groups, quads, per = PHASES[name]
                return groups // per, per, quads, UNIT0[name], GROUP0[name]

            for c in range(4):
                act.wait_ge(x_in[c], 16)
                fn(xsq[:, 4 * c:4 * c + 4, :], xin[:, 4 * c:4 * c + 4, :], ACTF.Square).then_inc(xsq_ready, 1)
            for n in range(RING):
                split_hi(n)
            act.wait_ge(ns_ready, 1)
            root(D_MODEL, rs_ready)
            norm_hi(0)

            for j in range(4):
                split_hi(RING + j)
            take_hsum(0, 4)
            act.wait_ge(parm_in, 32)
            fn(dtp[0:HEADS, 2:3], dtp[0:HEADS, 1:2], ACTF.Exp).then_inc(dt_exp, 1)
            act.wait_ge(dt_in, 1)
            fn(dtw[0:HEADS, 2, :], dtw[0:HEADS, 1, :], ACTF.Exp).then_inc(dt_exp, 1)
            act.wait_ge(th_ready, 1)
            fn(s5p[:, 9, :], s5k[:, 0, :], ACTF.Sin, scale=TWO_PI).then_inc(sincos, 1)
            fn(s5p[:, 10, :], s5k[:, 0, :], ACTF.Sin, scale=TWO_PI / 2).then_inc(sincos, 1)

            turns, per, quads, u0, g0 = phase("u")
            with act.Fori(0, turns) as i:
                for r in range(per):
                    for j in range(quads):
                        split_hi(u0 + r * quads + j + RING, i * (per * quads))
                    take_hsum(g0 + r, u0 + (r + 1) * quads, i * per, i * (per * quads))

            for name, blk0 in (("z", 0), ("x", 3), ("bc", 6)):
                turns, per, quads, u0, g0 = phase(name)
                with act.Fori(0, turns) as i:
                    for r in range(per):
                        split_hi(u0 + r * quads + RING, i * (per * quads))
                        act.wait_ge(ang_ready, i * 4 + (4 * blk0 + r + 1))
                        fn(tab[:, :, :], ang[:, :, :], ACTF.Sin, scale=TWO_PI).then_inc(tab_ready, 1)
                        for j in range(1, quads):
                            split_hi(u0 + r * quads + j + RING, i * (per * quads))
                        take_hsum(g0 + r, u0 + (r + 1) * quads, i * per, i * (per * quads))
                        if name == "z":
                            act.wait_ge(sum_ready, i * per + (g0 + r + 1))
                            to = zx[:, ds(i * 8 + 2 * r, 2), 0, :]
                            fn(to, to, ACTF.Silu).then_inc(z_done, 1)
                        else:
                            act.wait_ge(conv_done, i * per + (g0 - GROUP0["x"] + r + 1))
                            to = zx[:, ds(i * 8 + 2 * r, 2), 1, :] if name == "x" else (
                                bc[:, ds(i * 4 + r, 1), :, :].rearrange("p o c n -> p (o c) n"))
                            fn(to, to, ACTF.Silu).then_inc(xbc_done, 1)

            turns, per, quads, u0, g0 = phase("gate")
            act.wait_ge(xbc_done, 20)
            act.wait_ge(z_done, 12)
            with act.Fori(0, turns) as i:
                step.enter(i, 1)

                def hi(j):
                    split_hi(u0 + j + RING, i * 8)

                def decay(half):
                    act.wait_ge(scan_ready, i * 2 + (half + 1))
                    fn(dec[half][:, :, :], dec[half][:, :, :], ACTF.Exp).then_inc(exp_ready, 1)

                xg = zx[:, ds(i * TPG, TPG), 1, :]
                fn(bst[:, :], bc[:, ds(i, 1), 0, :].rearrange("p o n -> p (o n)"), ACTF.Copy).then_inc(staged, 1)
                fn(xst[:, :, :], xg, ACTF.Copy).then_inc(staged, 1)
                hi(0)
                hi(1)
                decay(0)
                hi(2)
                hi(3)
                take_hsum(g0, u0 + 4, i * 2, i * 8)
                hi(4)
                decay(1)
                hi(5)
                hi(6)
                act.wait_ge(yz_ready, i + 1)
                act.nop(nofuse=True)
                fn(xst[:, :, :], xg, ACTF.Square).then_inc(ysq_ready, 1)
                hi(7)
                take_hsum(g0 + 1, u0 + 8, i * 2, i * 8)
                act.wait_ge(yns_ready, i + 1)
                root(TPG * P, yrs_ready)
                act.wait_ge(yv_ready, i + 1)
                fn(y_hl[:, ds(i * TPG, TPG), 0:L], xg, ACTF.Copy).then_inc(yhi_ready, 1)
                step.leave(turns)

            act.wait_ge(y5_out, 8)
            fn(ub[:, :, :], ub[:, :, :], ACTF.Gelu_apprx_tanh).then_inc(y5_gelu, 1)
            act.wait_ge(y5_gelu, 1)
            act.wait_ge(ylo_ready, 8)
            fn(yb_hl[:, :, 0:L], ub[:, :, :], ACTF.Copy).then_inc(y5_hi, 1)
            act.wait_ge(sum_ready, GROUP0["proj"])

            turns, per, quads, u0, g0 = phase("proj")
            with act.Fori(0, turns) as i:
                for r in range(per):
                    to = gates[:, ds(i * 4 + 2 * r, 2), :]
                    fn(to, to, ACTF.Sigmoid).then_inc(ga_sig, 1)
                    for j in range(quads):
                        split_hi(u0 + r * quads + j + RING, i * (per * quads))
                    take_hsum(g0 + r, u0 + (r + 1) * quads, i * per, i * (per * quads))

            turns, per, quads, u0, g0 = phase("glu")
            with act.Fori(0, turns) as i:
                for r in range(per):
                    to = gates[:, ds(i * 2 + (16 + r), 1), :]
                    fn(to, to, ACTF.Sigmoid).then_inc(gb_sig, 1)
                    for j in range(quads):
                        split_hi(u0 + r * quads + j + RING, i * (per * quads))
                    take_hsum(g0 + r, u0 + (r + 1) * quads, i * per, i * (per * quads))
                    act.wait_ge(sum_ready, i * per + (g0 + r + 1))
                    fn(tsum[:, 1, :], tsum[:, 1, :], ACTF.Sigmoid).then_inc(glu_sig, 1)
                    act.wait_ge(m_sum, i * per + (r + 1))
                    fn(act16[:, ds(i * 2 + r, 1), 0:L], gates[:, ds(i * 2 + r, 1), :], ACTF.Copy).then_inc(m_hi, 1)

            def residual_phase(name, n, i, r, last=False):
                groups, quads, per = PHASES[name]
                u0, g0 = UNIT0[name], GROUP0[name]
                for j in range(quads):
                    if not (last and r == per - 1 and j >= quads - RING):
                        split_hi(u0 + r * quads + j + RING, i * (per * quads))
                take_hsum(g0 + r, u0 + (r + 1) * quads, i * per, i * (per * quads))
                act.wait_ge(sum_ready, i * per + (g0 + r + 1))
                act.wait_ge(sqacc_ready, i * per + (9 * n + r + 1))
                fn(sq[:, :, :], h[:, ds(i * (2 * per) + 2 * r, 2), :], ACTF.Square).then_inc(sq_ready, 1)

            with act.Fori(0, 4) as i:
                for r in range(2):
                    residual_phase("out", 0, i, r)
            act.wait_ge(ns_ready, 2)
            root(D_MODEL, rs_ready)
            norm_hi(1)

            turns, per, quads, u0, g0 = phase("up")
            with act.Fori(0, turns) as i:
                for r in range(per):
                    for j in range(quads):
                        split_hi(u0 + r * quads + j + RING, i * (per * quads))
                    take_hsum(g0 + r, u0 + (r + 1) * quads, i * per, i * (per * quads))
                    act.wait_ge(conv2_done, i * per + (r + 1))
                    fn(tsum[:, 0, :], tsum[:, 0, :], ACTF.Silu).then_inc(silu2_done, 1)
                    act.wait_ge(f_sum, i * per + (r + 1))
                    fn(ff[:, ds(i * 2 + r, 1), 0:L], tsum[:, 0:1, :], ACTF.Copy).then_inc(f_hi, 1)

            for i in range(2):
                for r in range(4):
                    residual_phase("down", 1, i, r, last=i == 1)
            act.wait_ge(ns_ready, 3)
            root(D_MODEL, rs_ready)

        @block.vector
        def _(dve):
            step = Tally(dve, dve_step)
            V = nc.vector

            def split_lo(n, ahead=0):
                s = n % RING
                dve.wait_ge(hi_ready, ahead + (n + 1))
                V.tensor_tensor(wlo[:, s, :], raw[:, s, :], whi[:, s, :], ALU.subtract).then_inc(lo_ready, 1)

            def add_halves(to, g, gi=0):
                dve.wait_ge(hsum_ready, gi + (g + 1))
                V.tensor_tensor(to, sums(g, 0), hsum[:, :, :], ALU.add).then_inc(sum_ready, 1)

            def norm_values(name, src, n, split=True):
                dve.wait_ge(rs_ready, n + 1)

                def lo(c):
                    dve.wait_ge(vhi_ready, 4 * n + c + 1)
                    k = slice(4 * c, 4 * c + 4)
                    V.tensor_tensor(act16[:, k, L:2 * L], vn[:, k, :], act16[:, k, 0:L],
                                    ALU.subtract).then_inc(vlo_ready, 1)
                for c in range(4):
                    for k in range(4 * c, 4 * c + 4):
                        ins = V.scalar_tensor_tensor(vn[:, k, :], src[:, k, :], col(name, k), rs[:, :],
                                                     ALU.mult, ALU.mult)
                    ins.then_inc(v_ready, 1)
                    if split and c:
                        lo(c - 1)
                if split:
                    lo(3)

            def horner(to, x, coefs):
                step.done(V.tensor_scalar(to, x, coefs[0], None, ALU.mult))
                for c in coefs[1:]:
                    step.done(V.scalar_tensor_tensor(to, to, c, x, ALU.add, ALU.mult))

            def mul(to, x, y, op=ALU.mult):
                step.done(V.tensor_tensor(to, x, y, op))

            for n in range(RING):
                split_lo(n)
            dve.wait_ge(parm_in, 32)
            norm_values("norm_mix", xin, 0)

            for j in range(4):
                split_lo(RING + j)
            add_halves(tsum[:, :, :], 0)
            dve.wait_ge(sum_ready, 1)
            d = [dtw[0:HEADS, k, :] for k in range(7)]
            step.done(V.tensor_scalar(d[0], tsum[0:HEADS, 0, :], dtp[0:HEADS, 0:1], None, ALU.add))
            V.scalar_tensor_tensor(d[1], d[0], -1.0, d[0], ALU.mult, ALU.min).then_inc(dt_in, 1)
            dve.wait_ge(dt_exp, 2)
            step.done(V.tensor_scalar(d[3], d[2], 2.0, None, ALU.add))
            step.done(V.reciprocal(d[3], d[3]))
            mul(d[3], d[3], d[2])
            mul(d[4], d[3], d[3])
            horner(d[5], d[4], [1.0 / k for k in (13, 11, 9, 7, 5, 3)])
            step.done(V.scalar_tensor_tensor(d[5], d[5], 1.0, d[3], ALU.add, ALU.mult))
            step.done(V.tensor_scalar(d[0], d[0], 0.0, None, ALU.max))
            step.done(V.scalar_tensor_tensor(d[6], d[5], 2.0, d[0], ALU.mult, ALU.add))
            V.tensor_scalar(d[5], d[6], dtp[0:HEADS, 2:3], -1.0, ALU.mult, ALU.mult).then_inc(dt_row, 1)

            s = [s5p[:, k, :] for k in range(20)]
            lam_im, angle, modulus = s5in[:, 1, :], s5k[:, 0, :], s5k[:, 1, :]
            dve.wait_ge(s5_in, 32)
            dve.wait_ge(const_ready, 9)
            step.done(V.tensor_copy(iota[:, :], iotai[:, :]))
            step.done(V.tensor_scalar(s[0], s5in[:, 0, :], EIG_MAX, None, ALU.min))
            step.done(V.tensor_scalar(s[1], s5in[:, 2, :], -87.0, 88.0, ALU.max, ALU.min))
            step.done(V.tensor_scalar(s[2], s[1], LOG2E, MAGIC, ALU.mult, ALU.add))
            step.done(V.tensor_scalar(s[2], s[2], MAGIC, None, ALU.subtract))
            step.done(V.scalar_tensor_tensor(s[1], s[2], -LN2_HI, s[1], ALU.mult, ALU.add))
            step.done(V.scalar_tensor_tensor(s[1], s[2], -LN2_LO, s[1], ALU.mult, ALU.add))
            horner(s[3], s[1], [1.0 / math.factorial(k) for k in range(7, 0, -1)])
            step.done(V.tensor_scalar(s5i[:, :], s[2], 127.0, 8388608.0, ALU.add, ALU.mult))
            step.done(V.scalar_tensor_tensor(s[4], s[3], 1.0, s5i[:, :].bitcast(F32), ALU.add, ALU.mult))
            mul(s[6], lam_im, s[4])
            step.done(V.tensor_scalar(s[6], s[6], 1.0 / (2 * math.pi), None, ALU.mult))
            step.done(V.tensor_scalar(s[7], s[6], MAGIC, None, ALU.add))
            step.done(V.tensor_scalar(s[7], s[7], MAGIC, None, ALU.subtract))
            mul(s[6], s[6], s[7], ALU.subtract)
            V.tensor_scalar(angle, s[6], 0.5, -0.5, ALU.min, ALU.max).then_inc(th_ready, 1)
            mul(s[5], s[0], s[4])
            step.done(V.tensor_scalar(s[5], s[5], -88.0, 1.0 / 256, ALU.max, ALU.mult))
            horner(s[8], s[5], [1.0 / math.factorial(k) for k in range(6, 0, -1)])
            for _ in range(8):
                step.done(V.scalar_tensor_tensor(s[8], s[8], 2.0, s[8], ALU.add, ALU.mult))
            step.done(V.tensor_scalar(modulus, s[8], 1.0, None, ALU.add))
            dve.wait_ge(sincos, 2)
            step.done(V.scalar_tensor_tensor(s[11], s[10], 2.0, s[10], ALU.mult, ALU.mult))
            mul(s[12], modulus, s[11])
            mul(s[12], s[8], s[12], ALU.subtract)
            mul(s[13], modulus, s[9])
            mul(s[14], s[0], s[0])
            mul(s[15], lam_im, lam_im)
            mul(s[14], s[14], s[15], ALU.add)
            step.done(V.reciprocal(s[15], s[14]))
            mul(s[16], s[12], s[0])
            mul(s[17], s[13], lam_im)
            mul(s[16], s[16], s[17], ALU.add)
            mul(s[16], s[16], s[15])
            mul(s[18], s[13], s[0])
            mul(s[19], s[12], lam_im)
            mul(s[18], s[18], s[19], ALU.subtract)
            mul(s[18], s[18], s[15])
            def wide(k):
                return s5p[:, k:k + 1, :].rearrange("p o j -> p j o").to_broadcast([P, S5T, 16])
            cr, ci, t0, t1 = craw[:, 0], craw[:, 1], ctmp[:, 0], ctmp[:, 1]
            mul(t0, cr, wide(16))
            mul(t1, ci, wide(18))
            mul(cfold[:, 0], t0, t1, ALU.subtract)
            mul(t0, cr, wide(18))
            mul(t1, ci, wide(16))
            step.done(V.scalar_tensor_tensor(cfold[:, 1], t0, -1.0, t1, ALU.mult, ALU.subtract))

            def phase(name):
                groups, quads, per = PHASES[name]
                return groups // per, per, quads, UNIT0[name], GROUP0[name]

            turns, per, quads, u0, g0 = phase("u")
            with dve.Fori(0, turns) as i:
                for r in range(per):
                    for j in range(quads):
                        split_lo(u0 + r * quads + j + RING, i * (per * quads))
                    add_halves(ub[:, ds(i * 4 + 2 * r, 2), :], g0 + r, i * per)
            dve.wait_ge(dt_T, 1)
            V.tensor_copy(dtt[:, :, :], DTT).then_inc(dt_v, 1)

            def s5_angles(tile):
                f = s5k[:, 0, ds(tile, 1)]
                V.tensor_scalar(ang[:, 0, :], iota[:, :], f, None, ALU.mult)
                step.done(V.tensor_scalar(ang[:, 1, :], iota[:, :], f, 0.25, ALU.mult, ALU.add))
                step.done(V.tensor_scalar(rot1[:, :, :], ang[:, :, :], MAGIC, MAGIC, ALU.add, ALU.subtract))
                V.tensor_tensor(ang[:, :, :], ang[:, :, :], rot1[:, :, :], ALU.subtract).then_inc(ang_ready, 1)

            sin2, cos2 = (tab[:, k:k + 1, :].to_broadcast([P, 2, L]) for k in range(2))

            def s5_scan(tile, count):
                dve.wait_ge(tab_ready, count)
                dve.wait_ge(bu_ready, count)
                V.tensor_tensor(rot1[:, :, :], BU, cos2, ALU.mult)
                mul(rot2[:, :, :], BU, sin2)
                V.tensor_tensor(st[:, 0, :], rot1[:, 0, :], rot2[:, 1, :], ALU.add)
                mul(st[:, 1, :], rot1[:, 1, :], rot2[:, 0, :], ALU.subtract)
                m = s5k[:, 1, ds(tile, 1)].to_broadcast([P, L])
                V.tensor_tensor_scan(rot1[:, 0, :], m, st[:, 0, :], 0.0, ALU.mult, ALU.add)
                step.done(V.tensor_tensor_scan(rot1[:, 1, :], m, st[:, 1, :], 0.0, ALU.mult, ALU.add))

            def s5_states():
                V.tensor_tensor(rot2[:, :, :], rot1[:, :, :], cos2, ALU.mult)
                mul(ang[:, :, :], rot1[:, :, :], sin2)
                V.tensor_tensor(st[:, 0, :], rot2[:, 0, :], ang[:, 1, :], ALU.subtract)
                V.tensor_tensor(st[:, 1, :], rot2[:, 1, :], ang[:, 0, :], ALU.add).then_inc(x5_ready, 1)

            def conv(to, tile, taps, w, b, t):
                pad = cpad[:, t, :]
                last = 3
                step.done(V.tensor_scalar(to, pad[:, last:last + L], col(w, tile * taps + (taps - 1)), col(b, tile),
                                          ALU.mult, ALU.add))
                for k in range(taps - 1):
                    off = last - (taps - 1) + k
                    ins = V.scalar_tensor_tensor(to, pad[:, off:off + L], col(w, tile * taps + k), to,
                                                 ALU.mult, ALU.add)
                    if k < taps - 2:
                        step.done(ins)
                return ins

            for name, blk0 in (("z", 0), ("x", 3), ("bc", 6)):
                turns, per, quads, u0, g0 = phase(name)
                with dve.Fori(0, turns) as i:
                    step.enter(i, 4 * 6 + (0 if name == "z" else 4 * 7))
                    for r in range(per):
                        tile = i * 4 + (4 * blk0 + r)
                        if r == 0:
                            dve.wait_ge(bu_ready, i * 4 + (4 * blk0 + 1))
                            for g in range(2):
                                rows = slice(64 * g, 64 * g + 64)
                                ins = V.tensor_copy(
                                    cz[rows, :, :, 16 * g:16 * g + 16],
                                    cfold[rows, :, ds(tile, 4), :].rearrange("p c r n -> p r c n"))
                            ins.then_inc(cz_ready, 1)
                        s5_angles(tile)
                        split_lo(u0 + r * quads + RING, i * (per * quads))
                        s5_scan(tile, i * 4 + (4 * blk0 + r + 1))
                        split_lo(u0 + r * quads + 1 + RING, i * (per * quads))
                        s5_states()
                        for j in range(2, quads):
                            split_lo(u0 + r * quads + j + RING, i * (per * quads))
                        dve.wait_ge(x5_ready, i * 4 + (4 * blk0 + r + 1))
                        if name == "z":
                            add_halves(zx[:, ds(i * 8 + 2 * r, 2), 0, :], g0 + r, i * per)
                            continue
                        add_halves(cpad[:, :, 3:3 + L], g0 + r, i * per)
                        dve.wait_ge(sum_ready, i * per + (g0 + r + 1))
                        for t in range(2):
                            q = i * 8 + (2 * r + t)
                            if name == "x":
                                to = zx[:, ds(q, 1), 1, :].rearrange("p o n -> p (o n)")
                            else:
                                to = bc[:, ds(i * 4 + r, 1), t, :].rearrange("p o n -> p (o n)")
                                q = i * 8 + (24 + 2 * r + t)
                            ins = conv(to, q, 4, "conv_a_w", "conv_a_b", t)
                            if t == 0:
                                step.done(ins)
                        ins.then_inc(conv_done, 1)
                    dve.wait_ge(y5_ready, i * 4 + (4 * blk0 + 4))
                    blk = i + blk0
                    to = ub[:, ds(blk, 1), :].rearrange("p o n -> p (o n)")
                    V.scalar_tensor_tensor(to, to, col("s5_d", blk), YS5, ALU.mult, ALU.add).then_inc(y5_out, 1)
                    dve.wait_ge(y5_out, i + (blk0 + 1))
                    step.leave(turns)

            turns, per, quads, u0, g0 = phase("gate")
            dve.wait_ge(z_done, 12)
            dve.wait_ge(xbc_done, 20)
            with dve.Fori(0, turns) as i:
                step.enter(i, 2)

                def lo(j):
                    split_lo(u0 + j + RING, i * 8)

                def scan(half):
                    dve.wait_ge(dec_in[half], i * 32 + 32)
                    for k in range(HALF):
                        ins = V.tensor_tensor_scan(dec[half][:, k, :], dec[half][:, k, :], mask[:, :], 0.0,
                                                   ALU.add, ALU.mult)
                    ins.then_inc(scan_ready, 1)

                def blocks(half):
                    dve.wait_ge(exp_ready, i * 2 + (half + 1))
                    V.tensor_tensor(dec[half][:, :, :], dec[half][:, :, :],
                                    cbm[:, :].rearrange("p (o n) -> p o n", o=1).to_broadcast([P, HALF, ML]),
                                    ALU.mult).then_inc(m_ready, 1)

                q = ds(i * TPG, TPG)
                lo(0)
                dve.wait_ge(cb_ready, i + 1)
                V.tensor_tensor(cbm[:, :], CB, mask_in[:, :], ALU.mult)
                dve.wait_ge(xp_ready, i + 1)
                for k in range(2):
                    ins = V.tensor_tensor(
                        xtok[:, k, :].rearrange("p (h n) -> p h n", h=HPG), XP[k].rearrange("p (h n) -> p h n", h=HPG),
                        dtt[:, k, ds(i * HPG, HPG)].rearrange("p (h o) -> p h o", o=1).to_broadcast([P, HPG, 64]),
                        ALU.mult)
                step.done(ins)
                lo(1)
                scan(0)
                lo(2)
                blocks(0)
                lo(3)
                add_halves(gates[:, ds(i * 4, 2), :], g0, i * 2)
                lo(4)
                scan(1)
                lo(5)
                blocks(1)
                lo(6)
                dve.wait_ge(y_ready, i * 2 + 2)
                for k in range(TPG):
                    x = zx[:, ds(i * TPG + k, 1), 1, :].rearrange("p o n -> p (o n)")
                    ins = V.scalar_tensor_tensor(x, x, col("d_a", i * TPG + k), YY[k], ALU.mult, ALU.add)
                step.done(ins)
                V.tensor_tensor(zx[:, q, 1, :], zx[:, q, 1, :], zx[:, q, 0, :], ALU.mult).then_inc(yz_ready, 1)
                lo(7)
                add_halves(gates[:, ds(i * 4 + 2, 2), :], g0 + 1, i * 2)
                dve.wait_ge(yrs_ready, i + 1)
                for k in range(TPG):
                    x = zx[:, ds(i * TPG + k, 1), 1, :].rearrange("p o n -> p (o n)")
                    ins = V.scalar_tensor_tensor(x, x, col("norm_a", i * TPG + k), rs[:, :], ALU.mult, ALU.mult)
                ins.then_inc(yv_ready, 1)
                dve.wait_ge(yhi_ready, i + 1)
                V.tensor_tensor(y_hl[:, q, L:2 * L], zx[:, q, 1, :], y_hl[:, q, 0:L],
                                ALU.subtract).then_inc(ylo_ready, 1)
                step.leave(turns)

            dve.wait_ge(y5_hi, 1)
            V.tensor_tensor(yb_hl[:, :, L:2 * L], ub[:, :, :], yb_hl[:, :, 0:L], ALU.subtract).then_inc(y5_lo, 1)

            turns, per, quads, u0, g0 = phase("proj")
            with dve.Fori(0, turns) as i:
                step.enter(i, 2)
                for r in range(per):
                    for j in range(quads):
                        split_lo(u0 + r * quads + j + RING, i * (per * quads))
                    add_halves(tsum[:, :, :], g0 + r, i * per)
                    dve.wait_ge(sum_ready, i * per + (g0 + r + 1))
                    dve.wait_ge(ga_sig, i * per + (r + 1))
                    to = gates[:, ds(i * 4 + 2 * r, 2), :]
                    mul(to, tsum[:, :, :], to)
                step.leave(turns)

            turns, per, quads, u0, g0 = phase("glu")
            with dve.Fori(0, turns) as i:
                step.enter(i, 4)
                for r in range(per):
                    for j in range(quads):
                        split_lo(u0 + r * quads + j + RING, i * (per * quads))
                    add_halves(tsum[:, :, :], g0 + r, i * per)
                    dve.wait_ge(glu_sig, i * per + (r + 1))
                    mul(tsum[:, 0, :], tsum[:, 0, :], tsum[:, 1, :])
                    gb, ga = gates[:, ds(i * 2 + (16 + r), 1), :], gates[:, ds(i * 2 + r, 1), :]
                    mul(tsum[:, 0:1, :], tsum[:, 0:1, :], gb)
                    V.tensor_tensor(ga, ga, tsum[:, 0:1, :], ALU.add).then_inc(m_sum, 1)
                    dve.wait_ge(m_hi, i * per + (r + 1))
                    to = act16[:, ds(i * 2 + r, 1), :]
                    V.tensor_tensor(to[:, :, L:2 * L], ga, to[:, :, 0:L], ALU.subtract).then_inc(m_lo, 1)
                step.leave(turns)

            def residual_phase(name, i, r, last=False):
                groups, quads, per = PHASES[name]
                u0, g0 = UNIT0[name], GROUP0[name]
                for j in range(quads):
                    if not (last and r == per - 1 and j >= quads - RING):
                        split_lo(u0 + r * quads + j + RING, i * (per * quads))
                hg = h[:, ds(i * (2 * per) + 2 * r, 2), :]
                dve.wait_ge(hsum_ready, i * per + (g0 + r + 1))
                mul(hg, hg, hsum[:, :, :], ALU.add)
                V.tensor_tensor(hg, sums(g0 + r, 0), hg, ALU.add).then_inc(sum_ready, 1)

            dve.wait_ge(h_in, 16)
            with dve.Fori(0, 4) as i:
                step.enter(i, 2)
                for r in range(2):
                    residual_phase("out", i, r)
                step.leave(4)
            dve.wait_ge(sum_ready, GROUP0["up"])
            norm_values("norm_ffn", h, 1)

            turns, per, quads, u0, g0 = phase("up")
            with dve.Fori(0, turns) as i:
                step.enter(i, 10)
                for r in range(per):
                    for j in range(quads):
                        split_lo(u0 + r * quads + j + RING, i * (per * quads))
                    add_halves(cpad[:, :, 3:3 + L], g0 + r, i * per)
                    dve.wait_ge(sum_ready, i * per + (g0 + r + 1))
                    for t in range(2):
                        ins = conv(tsum[:, t, :], i * 4 + (2 * r + t), 3, "conv_f_w", "conv_f_b", t)
                        if t == 0:
                            step.done(ins)
                    ins.then_inc(conv2_done, 1)
                    dve.wait_ge(silu2_done, i * per + (r + 1))
                    V.tensor_tensor(tsum[:, 0, :], tsum[:, 0, :], tsum[:, 1, :], ALU.mult).then_inc(f_sum, 1)
                    dve.wait_ge(f_hi, i * per + (r + 1))
                    to = ff[:, ds(i * 2 + r, 1), :]
                    V.tensor_tensor(to[:, :, L:2 * L], tsum[:, 0:1, :], to[:, :, 0:L], ALU.subtract).then_inc(f_lo, 1)
                    dve.wait_ge(f_lo, i * per + (r + 1))
                step.leave(turns)

            for i in range(2):
                for r in range(4):
                    residual_phase("down", i, r, last=i == 1)
            dve.wait_ge(sum_ready, N_ALL)
            norm_values("norm_final", h, 2, split=False)

        @block.tensor
        def _(pe):
            mm = nc.tensor.matmul

            def unit(name, r, q, act, i=0):
                groups, quads, per = PHASES[name]
                n, g = UNIT0[name] + r * quads + q, GROUP0[name] + r
                pe.wait_ge(lo_ready, i * (per * quads) + (n + 1))
                if q == 0 and g >= 1:
                    pe.wait_ge(sum_ready, i * per + (g - 1 if g >= 2 else g))
                s, b = n % RING, 2 * (g % 2)
                for k in range(4):
                    x = act[:, 4 * q + k, :]
                    first, last = q == 0 and k == 0, q == quads - 1 and k == 3
                    for t in range(2):
                        cols = slice(k * L + t * P, k * L + t * P + P)
                        mm(psum[:, b + t, :], whi[:, s, cols], x, start=first, stop=False)
                        ins = mm(psum[:, b + t, L:2 * L], wlo[:, s, cols], x[:, 0:L], start=False, stop=last)
                ins.then_inc(unit_used, 1)

            def ones_sum(parts):
                for k, x in enumerate(parts):
                    ins = mm(NS, ones[:, :], x, start=k == 0, stop=k == len(parts) - 1)
                return ins

            pe.wait_ge(const_ready, 1)
            for k in range(KT):
                if k % 4 == 0:
                    pe.wait_ge(xsq_ready, k // 4 + 1)
                ins = mm(NS, ones[:, :], xsq[:, k, :], start=k == 0, stop=k == KT - 1)
            ins.then_inc(ns_ready, 1)

            for q in range(4):
                pe.wait_ge(vlo_ready, q + 1)
                unit("dt", 0, q, act16)
            with pe.Fori(0, 2) as i:
                for r in range(2):
                    for q in range(4):
                        unit("u", r, q, act16, i)
            pe.wait_ge(const_ready, 9)
            pe.wait_ge(dt_row, 1)
            for k in range(2):
                ins = nc.tensor.transpose(DTT[:, k, :], dtw[0:HEADS, 6, k * P:k * P + P], ident[0:HEADS, 0:HEADS])
            ins.then_inc(dt_T, 1)
            pe.wait_ge(sum_ready, GROUP0["z"])
            for name, blk0 in (("z", 0), ("x", 3), ("bc", 6)):
                with pe.Fori(0, PHASES[name][0] // 4) as i:
                    for r in range(4):
                        pe.wait_ge(b_in[r], i * 32 + 32 * (blk0 + 1))
                        for k in range(2):
                            ins = mm(BU[:, k, :], bz[:, r, k, :],
                                     ub[:, ds(i + blk0, 1), :].rearrange("p o n -> p (o n)"), start=True, stop=True)
                        ins.then_inc(bu_ready, 1)
                        for q in range(4):
                            unit(name, r, q, act16, i)
                        pe.wait_ge(cz_ready, i + (blk0 + 1))
                        pe.wait_ge(x5_ready, i * 4 + (4 * blk0 + r + 1))
                        for k in range(2):
                            ins = mm(YS5[32 * r:32 * r + 32], cz[:, r, k, :], st[:, k, :], start=k == 0, stop=k == 1)
                        ins.then_inc(y5_ready, 1)

            pe.wait_ge(y5_out, 8)
            with pe.Fori(0, GROUPS) as i:
                def heads(half):
                    pe.wait_ge(m_ready, i * 2 + (half + 1))
                    for k in range(HALF):
                        hd = half * HALF + k
                        y = YY[hd // 2][64 * (hd % 2):64 * (hd % 2) + 64]
                        x = slice(64 * hd, 64 * hd + 64)
                        mm(y, xtok[:, 0, x], dec[half][:, k, 0:L], start=True, stop=False)
                        ins = mm(y[:, P:L], xtok[:, 1, x], dec[half][:, k, L:ML], start=False, stop=True)
                    ins.then_inc(y_ready, 1)

                pe.wait_ge(staged, i * 2 + 2)
                c = bc[:, ds(i, 1), 1, :].rearrange("p o n -> p (o n)")
                mm(CB[:, 0:L], bst[:, 0:P], c, start=True, stop=True)
                mm(CB[:, L:ML], bst[:, P:L], c[:, P:L], start=True, stop=True).then_inc(cb_ready, 1)
                for k in range(2):
                    for t in range(TPG):
                        ins = nc.tensor.transpose(XP[k][:, t * P:t * P + P], xst[:, t, k * P:k * P + P], ident[:, :])
                ins.then_inc(xp_ready, 1)
                for q in range(4):
                    unit("gate", 0, q, act16, i)
                heads(0)
                for q in range(2):
                    unit("gate", 1, q, act16, i)
                heads(1)
                for q in range(2, 4):
                    unit("gate", 1, q, act16, i)
                pe.wait_ge(ysq_ready, i + 1)
                ones_sum([xst[:, t, :] for t in range(TPG)]).then_inc(yns_ready, 1)

            for name, src, ready, value in (("proj", y_hl, ylo_ready, 8), ("glu", yb_hl, y5_lo, 1),
                                            ("out", act16, m_lo, 16), ("up", act16, None, 0),
                                            ("down", ff, f_lo, 44)):
                groups, quads, per = PHASES[name]
                if name == "up":
                    pe.wait_ge(sqacc_ready, 9)
                    ones_sum([sqacc[:, k, :] for k in range(2)]).then_inc(ns_ready, 1)
                else:
                    pe.wait_ge(ready, value)
                with pe.Fori(0, groups // per) as i:
                    for r in range(per):
                        for q in range(quads):
                            if name == "up" and r == 0:
                                pe.wait_ge(vlo_ready, 4 + q + 1)
                            unit(name, r, q, src, i)
            pe.wait_ge(sqacc_ready, 18)
            ones_sum([sqacc[:, k, :] for k in range(2)]).then_inc(ns_ready, 1)

    return nc


def _units(w):
    rows, cols = w.shape
    w = w.reshape(rows // 512, 4, P, cols // 256, 256).transpose(3, 0, 2, 1, 4)
    return np.ascontiguousarray(w).reshape(-1, P, UNIT)


def _pairs(x, y, width=P):
    lead = x.shape[:-1]
    x, y = x.reshape(*lead, -1, 1, width), y.reshape(*lead, -1, 1, width)
    return np.concatenate([x, y], axis=-2).reshape(*lead, -1)


def _tiles(v):
    return v.reshape(-1, P).T


def _conv(w):
    return w.reshape(w.shape[0], -1, P).transpose(2, 1, 0).reshape(P, -1)


def kernel(**inputs):
    import concourse.bacc as bacc
    from concourse.bass_utils import run_bass_kernel_spmd

    v = {k: np.asarray(x) for k, x in inputs.items()}
    w_in = v["w_in"][0]
    cut = np.cumsum([0, D_INNER, D_INNER, 1024, 1024, HEADS, D_S5, 2 * D_MODEL])
    z, x, b, c, dt, u, gate = (w_in[:, cut[k]:cut[k + 1]] for k in range(7))
    glu, up = v["w_s5_glu"][0], v["w_up"][0]
    cw, cb, fw, fb = v["conv_a_w"][0], v["conv_a_b"][0], v["conv_ffn_w"][0], v["conv_ffn_b"][0]

    def xbc_order(m):
        return np.concatenate([m[..., :D_INNER], _pairs(m[..., D_INNER:D_INNER + 1024], m[..., D_INNER + 1024:])], axis=-1)

    def halves(m):
        n = m.shape[-1] // 2
        return _pairs(m[..., :n], m[..., n:])

    a = {
        "x": np.ascontiguousarray(v["x"][0].reshape(L, KT, P).transpose(2, 1, 0)),
        "w_dt": _units(w_in[:, cut[4]:cut[4] + 256]), "w_u": _units(u), "w_z": _units(z), "w_x": _units(x),
        "w_bc": _units(_pairs(b, c)), "w_gate": _units(gate), "w_proj": _units(v["w_proj_a"][0]),
        "w_glu": _units(halves(glu)), "w_out": _units(v["w_out"][0]), "w_up": _units(halves(up)),
        "w_down": _units(v["w_down"][0]),
        "dtp": np.ascontiguousarray(np.stack([v["dt_bias"][0], v["a_log"][0]], axis=1)),
        "s5_lam": np.ascontiguousarray(np.stack(
            [v["s5_lam_re"][0], v["s5_lam_im"][0],
             np.broadcast_to(v["s5_log_dt"][0][:, None], (64, 64))]).reshape(3, S5T, P).transpose(2, 0, 1)),
        "s5_c": np.ascontiguousarray(np.stack([v["s5_c_re"][0], v["s5_c_im"][0]])
                                     .transpose(0, 1, 3, 2).reshape(2, S5T, P, 16).transpose(2, 0, 1, 3)),
        "s5_b": np.ascontiguousarray(np.stack([v["s5_b_re"][0], v["s5_b_im"][0]]).transpose(1, 3, 0, 2)),
    }
    a["parm"] = np.ascontiguousarray(np.concatenate([
        _tiles(v["norm_mix_w"][0]), _tiles(v["norm_ffn_w"][0]), _tiles(v["norm_final_w"]), _tiles(v["norm_a_w"][0]),
        _tiles(np.repeat(v["d_a"][0], 64)), _conv(xbc_order(cw)), _tiles(xbc_order(cb)), _conv(halves(fw)),
        _tiles(halves(fb)), _tiles(v["s5_d"][0])], axis=1))

    nc = bacc.Bacc("TRN2", target_bir_lowering=False, num_devices=1)
    aps = {k: nc.dram_tensor(f"in_{k}", m.shape, mybir.dt.from_np(m.dtype), kind="ExternalInput").ap()
           for k, m in a.items()}
    out = nc.dram_tensor("out", (P, KT, L), F32, kind="ExternalOutput").ap()
    build_program(nc, aps, out)
    r = run_bass_kernel_spmd(nc, [{f"in_{k}": m for k, m in a.items()}], core_ids=[0])
    y = r.results[0]["out"]
    return np.ascontiguousarray(y.transpose(2, 1, 0)).reshape(1, L, D_MODEL)
```

```python
import math
from contextlib import ExitStack

import numpy as np
import concourse.bass as bass
from concourse import mybir

F32, F32R, I32 = mybir.dt.float32, mybir.dt.float32r, mybir.dt.int32
ALU, ACTF = mybir.AluOpType, mybir.ActivationFunctionType
ds = bass.ds

P = 128
L = 256
D_MODEL, D_INNER, D_S5, D_FF = 2048, 3072, 1024, 5632
HEADS, GROUPS = 48, 8
HPG = HEADS // GROUPS
HALF = HPG // 2
TPG = D_INNER // GROUPS // P
EPS, EIG_MAX = 1e-6, -1e-4
KT = D_MODEL // P
S5T = 32
RING = 4
UNIT = 4 * 256
ML = L + P

PHASES = {"dt": (1, 4, 1), "u": (4, 4, 2), "zx": (24, 4, 4), "bc": (8, 4, 4), "gate": (16, 4, 2),
          "proj": (8, 6, 2), "glu": (16, 2, 2), "out": (8, 4, 2), "up": (44, 4, 2), "down": (8, 11, 4)}
UNIT0, GROUP0, N_UNITS, N_ALL = {}, {}, 0, 0
for _n, (_g, _q, _b) in PHASES.items():
    UNIT0[_n], GROUP0[_n] = N_UNITS, N_ALL
    N_UNITS, N_ALL = N_UNITS + _g * _q, N_ALL + _g

PARM = {}
_at = 0
for _n, _w in (("norm_mix", 16), ("norm_ffn", 16), ("norm_final", 16), ("norm_a", 24), ("d_a", 24),
               ("conv_a_w", 160), ("conv_a_b", 40), ("conv_f_w", 264), ("conv_f_b", 88), ("s5_d", 8)):
    PARM[_n] = _at
    _at += _w
N_PARM = _at

LOG2E, LN2_HI, LN2_LO = 1.4426950408889634, 0.693359375, -2.12194440054690583e-4
MAGIC = 12582912.0
TWO_PI = 6.2831850


class Tally:

    def __init__(self, eng, sem):
        self.eng, self.sem, self.n, self.i, self.per, self.start = eng, sem, 0, None, 0, 0

    def enter(self, i, per, first=0):
        self.i, self.per, self.first, self.start = i, per, first, self.n

    def leave(self, turns):
        assert self.n - self.start == self.per, f"{self.n - self.start} steps in a turn, not {self.per}"
        self.i, self.n = None, self.start + (turns - self.first) * self.per

    def begun(self, ins):
        ins.then_inc(self.sem, 1)
        self.n += 1

    def hold(self, but=0):
        n = self.n - but
        self.eng.wait_ge(self.sem, n if self.i is None else self.i * self.per + (n - self.first * self.per))

    def done(self, ins):
        self.begun(ins)
        self.hold()


def build_program(nc, a, out):
    ctx = ExitStack()
    with ctx:
        base = nc.sbuf_base + -nc.sbuf_base % 64
        room = nc.sbuf_usable_end - base
        K = 1024

        def at(name, shape, dt, off):
            size = 4 * math.prod(shape[1:])
            assert off + size <= room, (name, off, size, room)
            return nc.alloc_sbuf_tensor_at(name, shape, dt, offset=base + off)

        raw = at("raw", [P, RING, UNIT], F32, 0)
        whi = at("whi", [P, RING, UNIT], F32R, 16 * K)
        wlo = at("wlo", [P, RING, UNIT], F32R, 32 * K)
        act16 = at("act16", [P, KT, 2 * L], F32R, 48 * K)
        zx = at("zx", [P, 24, 2, L], F32, 80 * K)
        y_hl = at("y_hl", [P, 24, 2 * L], F32R, 80 * K)
        vn = at("vn", [P, KT, L], F32, 80 * K)
        ff = at("ff", [P, 44, 2 * L], F32R, 80 * K)
        gates = at("gates", [P, 32, L], F32, 128 * K)
        bc = at("bc", [P, GROUPS, 2, L], F32, 152 * K)
        xin = at("xin", [P, KT, L], F32, 152 * K)
        ub = at("ub", [P, 8, L], F32, 168 * K)
        h = at("h", [P, KT, L], F32, 168 * K)
        yb_hl = at("yb_hl", [P, 8, 2 * L], F32R, 181 * K)
        tab = at("tab", [P, 2, L], F32, 128 * K)
        ang = at("ang", [P, 2, L], F32, 130 * K)
        rot1 = at("rot1", [P, 2, L], F32, 132 * K)
        rot2 = at("rot2", [P, 2, L], F32, 134 * K)
        st = at("st", [P, 2, L], F32, 136 * K)
        bz = at("bz", [P, 4, 2, P], F32, 138 * K)
        cz = at("cz", [P, 4, 2, 32], F32, 142 * K)
        cfold = at("cfold", [P, 2, S5T, 16], F32, 143 * K)
        iota = at("iota", [P, L], F32, 147 * K)
        angm = at("angm", [P, 2, L], F32, 149 * K)
        s5in = at("s5in", [P, 3, S5T], F32, 148 * K)
        craw = at("craw", [P, 2, S5T, 16], F32, 96 * K)
        ctmp = at("ctmp", [P, 2, S5T, 16], F32, 100 * K)
        s5p = at("s5p", [P, 20, S5T], F32, 104 * K)
        s5i = at("s5i", [P, S5T], I32, 107 * K)
        iotai = at("iotai", [P, L], I32, 108 * K)
        xsq = at("xsq", [P, KT, L], F32, 112 * K)
        W = 176 * K
        dec = [at(f"dec{k}", [P, HALF, ML], F32, W + k * 4608) for k in range(2)]
        xst = at("xst", [P, TPG, L], F32, W + 9216)
        xtok = at("xtok", [P, 2, HPG * 64], F32, W + 12288)
        cbm = at("cbm", [P, ML], F32, W + 15360)
        mask = at("mask", [P, ML], F32, W + 16896)
        mask_in = at("mask_in", [P, ML], F32, W + 18432)
        ident = at("ident", [P, P], F32, W + 19968)
        dtt = at("dtt", [P, 2, HEADS], F32, W + 20480)
        dtw = at("dtw", [P, 7, L], F32, W)
        C = W + 21 * K
        hsum = at("hsum", [P, 2, L], F32, C)
        tsum = at("tsum", [P, 2, L], F32, C + 2048)
        rot3 = at("rot3", [P, 2, L], F32, C + 2048)
        bst = at("bst", [P, L], F32, C + 2048)
        cpad = at("cpad", [P, 2, L + 4], F32, C + 4096)
        parm = at("parm", [P, N_PARM], F32, C + 6208)
        rs = at("rs", [P, L], F32, C + 8832)
        sq = at("sq", [P, 2, L], F32, 185 * K)
        sqacc = at("sqacc", [P, 2, L], F32, 187 * K)
        ones = at("ones", [P, P], F32, C + 9856)
        s5k = at("s5k", [P, 2, S5T], F32, C + 10368)
        dtp = at("dtp", [P, 3], F32, C + 10624)
        scr = nc.dram_tensor("decay_rows", (HEADS, L), F32).ap()

        psum = ctx.enter_context(nc.psum_tensor("psum", [P, 8, 512], F32))
        BU = [psum[:, b, :].rearrange("p (c n) -> p c n", c=2) for b in (4, 6)]
        YS5 = psum[:, 5, 0:L]
        CB, XP = psum[:, 4, 0:ML], [psum[:, 5, 0:ML], psum[:, 6, 0:ML]]
        YY = [psum[:, 7, 0:L], psum[:, 7, L:2 * L], psum[:, 4, 0:L]]
        NS = psum[:, 7, 0:L]
        DTT = psum[:, 5, 0:2 * HEADS].rearrange("p (s h) -> p s h", s=2)

        def sem(name):
            return ctx.enter_context(nc.semaphore(name))

        x_in, w_in, b_in = [[sem(f"{n}{k}") for k in range(4)] for n in ("x_in", "w_in", "b_in")]
        parm_in, s5_in, h_in, out_done, scr_w = map(sem, ("parm_in", "s5_in", "h_in", "out_done", "scr_w"))
        dec_in = [sem("dec_in0"), sem("dec_in1")]
        hi_ready, lo_ready, unit_used, hsum_ready, sum_ready = map(
            sem, ("hi_ready", "lo_ready", "unit_used", "hsum_ready", "sum_ready"))
        dve_step, act_step, pool_step, const_ready = map(sem, ("dve_step", "act_step", "pool_step", "const_ready"))
        xsq_ready, sq_ready, sqacc_ready, ns_ready, rs_ready, v_ready, vhi_ready, vlo_ready = map(
            sem, ("xsq_ready", "sq_ready", "sqacc_ready", "ns_ready", "rs_ready", "v_ready", "vhi_ready", "vlo_ready"))
        dt_in, dt_exp, dt_row, dt_T, dt_v = map(sem, ("dt_in", "dt_exp", "dt_row", "dt_T", "dt_v"))
        iota_ready, angm_ready = sem("iota_ready"), sem("angm_ready")
        th_ready, sincos, bu_ready, ang_ready, tab_ready, x5_ready, y5_ready, cz_ready, y5_out, y5_gelu, y5_hi, y5_lo = map(
            sem, ("th_ready", "sincos", "bu_ready", "ang_ready", "tab_ready", "x5_ready", "y5_ready", "cz_ready",
                  "y5_out", "y5_gelu", "y5_hi", "y5_lo"))
        z_done, conv_done, xbc_done, staged, cb_ready, xp_ready, scan_ready, exp_ready, m_ready, y_ready = map(
            sem, ("z_done", "conv_done", "xbc_done", "staged", "cb_ready", "xp_ready", "scan_ready", "exp_ready",
                  "m_ready", "y_ready"))
        yz_ready, ysq_ready, yns_ready, yrs_ready, yv_ready, yhi_ready, ylo_ready = map(
            sem, ("yz_ready", "ysq_ready", "yns_ready", "yrs_ready", "yv_ready", "yhi_ready", "ylo_ready"))
        ga_sig, gb_sig, glu_sig, m_sum, m_hi, m_lo, conv2_done, silu2_done, f_sum, f_hi, f_lo = map(
            sem, ("ga_sig", "gb_sig", "glu_sig", "m_sum", "m_hi", "m_lo", "conv2_done", "silu2_done", "f_sum",
                  "f_hi", "f_lo"))

        block = ctx.enter_context(nc.Block())

        def col(name, n):
            return parm[:, ds(n + PARM[name], 1)]

        def sums(g, half):
            b = 2 * (g % 2)
            return psum[:, b:b + 2, half * L:half * L + L]

        @block.sync
        def _(sp):
            for c in range(4):
                sp.dma_start(xin[:, 4 * c:4 * c + 4, :], a["x"][:, 4 * c:4 * c + 4, :]).then_inc(x_in[c], 16)
            for n in range(RING):
                sp.dma_start(raw[:, n, :], a["w_dt"][n]).then_inc(w_in[n], 16)
            sp.dma_start(parm[:, :], a["parm"]).then_inc(parm_in, 16)
            sp.dma_start(dtp[0:HEADS, 0:2], a["dtp"]).then_inc(parm_in, 16)
            sp.dma_start(s5in[:, :, :], a["s5_lam"]).then_inc(s5_in, 16)
            sp.dma_start(craw[:, :, :, :], a["s5_c"]).then_inc(s5_in, 16)
            for name in list(PHASES)[1:]:
                groups, quads, per = PHASES[name]
                with sp.Fori(0, groups // per) as i:
                    for j in range(per * quads):
                        n = UNIT0[name] + j
                        sp.wait_ge(lo_ready, i * (per * quads) + (n - RING + 1))
                        sp.dma_start(raw[:, n % RING, :],
                                     a["w_" + name][ds(i * (per * quads) + j, 1), :, :]
                                     .rearrange("o p n -> (o p) n")).then_inc(w_in[n % RING], 16)
            for c in range(4):
                sp.wait_ge(v_ready, 8 + c + 1)
                sp.dma_start(out[:, 4 * c:4 * c + 4, :], vn[:, 4 * c:4 * c + 4, :]).then_inc(out_done, 16)
            sp.wait_ge(out_done, 64)

        @block.gpsimd
        def _(pool):
            step = Tally(pool, pool_step)
            nc.gpsimd.memset(ones[:, :], 1.0).then_inc(const_ready, 1)
            step.done(nc.gpsimd.memset(bz[:, :, :, :], 0.0))

            def load_b(blk, r):
                for g in range(2):
                    pool.dma_start(bz[32 * r + 16 * g:32 * r + 16 * g + 16, r, :, 64 * g:64 * g + 64],
                                   a["s5_b"][ds(blk * 8 + (2 * r + g), 1), :, :, :]
                                   .rearrange("o c k n -> (o c) k n")).then_inc(b_in[r], 16)

            def load_decay(g, half):
                rows = scr[ds(g * HPG + half * HALF, HALF), :]
                for lo, off in ((0, 0), (P, L)):
                    pool.dma_start(dec[half][:, :, off:off + L - lo],
                                   rows[:, lo:L].rearrange("(o h) n -> o h n", o=1).to_broadcast([P, HALF, L - lo])
                                   ).then_inc(dec_in[half], 16)

            for r in range(4):
                load_b(0, r)
            nc.gpsimd.memset(cz[:, :, :, :], 0.0).then_inc(const_ready, 1)
            nc.gpsimd.memset(cpad[:, :, :], 0.0).then_inc(const_ready, 1)
            nc.gpsimd.iota(iotai[:, :], pattern=[[1, L]], base=0, channel_multiplier=0).then_inc(const_ready, 1)
            step.done(nc.gpsimd.memset(ident[:, :], 0.0))
            nc.gpsimd.affine_select(out=ident[:, :], in_=ident[:, :], compare_op=ALU.not_equal, fill=1.0, base=0,
                                    pattern=[[-1, P]], channel_multiplier=1).then_inc(const_ready, 1)
            for m, keep in ((mask, ALU.is_gt), (mask_in, ALU.is_ge)):
                step.done(nc.gpsimd.memset(m[:, :], 1.0))
                for off, width in ((0, L), (L, P)):
                    nc.gpsimd.affine_select(out=m[:, off:off + width], in_=m[:, off:off + width], compare_op=keep,
                                            fill=0.0, base=0, pattern=[[1, width]],
                                            channel_multiplier=-1).then_inc(const_ready, 1)
            pool.wait_ge(dt_row, 1)
            pool.dma_start(scr[:, :], dtw[0:HEADS, 5, :]).then_inc(scr_w, 16)
            with pool.Fori(0, 7) as i:
                for r in range(4):
                    pool.wait_ge(bu_ready, i * 4 + (r + 1))
                    load_b(i + 1, r)
            pool.wait_ge(scr_w, 16)
            pool.wait_ge(dt_v, 1)
            for half in range(2):
                load_decay(0, half)
            with pool.Fori(0, GROUPS - 1) as i:
                for half in range(2):
                    pool.wait_ge(y_ready, i * 2 + (half + 1))
                    load_decay(i + 1, half)
            pool.wait_ge(unit_used, UNIT0["out"])
            pool.dma_start(h[:, :, :], a["x"]).then_inc(h_in, 16)
            for n in range(2):
                pool.wait_ge(ns_ready, n + 1)
                pool.wait_ge(sum_ready, GROUP0["out" if n == 0 else "down"])
                nc.gpsimd.memset(sqacc[:, :, :], 0.0).then_inc(sqacc_ready, 1)
                with pool.Fori(0, 8) as i:
                    pool.wait_ge(sqacc_ready, i + (9 * n + 1))
                    pool.wait_ge(sq_ready, i + (8 * n + 1))
                    nc.gpsimd.tensor_tensor(sqacc[:, :, :], sqacc[:, :, :], sq[:, :, :],
                                            ALU.add).then_inc(sqacc_ready, 1)

        @block.scalar
        def _(act):
            step = Tally(act, act_step)
            fn = nc.scalar.activation

            def split_hi(n, ahead=0):
                s = n % RING
                act.wait_ge(w_in[s], ahead * (16 // RING) + 16 * (n // RING + 1))
                if n >= RING:
                    act.wait_ge(unit_used, ahead + (n - RING + 1))
                fn(whi[:, s, :], raw[:, s, :], ACTF.Copy).then_inc(hi_ready, 1)

            def take_hsum(g, end, gi=0, ui=0):
                act.wait_ge(unit_used, ui + end)
                if g:
                    act.wait_ge(sum_ready, gi + g)
                tiles = slice(0, 2 if g else 1)
                fn(hsum[:, tiles, :], sums(g, 1)[:, tiles, :], ACTF.Copy).then_inc(hsum_ready, 1)

            def root(count, to):
                step.done(fn(rs[:, :], NS, ACTF.Ln, bias=EPS, scale=1.0 / count))
                fn(rs[:, :], rs[:, :], ACTF.Exp, scale=-0.5).then_inc(to, 1)

            def norm_hi(n):
                for c in range(4):
                    act.wait_ge(v_ready, 4 * n + c + 1)
                    fn(act16[:, 4 * c:4 * c + 4, 0:L], vn[:, 4 * c:4 * c + 4, :], ACTF.Copy).then_inc(vhi_ready, 1)

            def phase(name):
                groups, quads, per = PHASES[name]
                return groups // per, per, quads, UNIT0[name], GROUP0[name]

            for c in range(4):
                act.wait_ge(x_in[c], 16)
                fn(xsq[:, 4 * c:4 * c + 4, :], xin[:, 4 * c:4 * c + 4, :], ACTF.Square).then_inc(xsq_ready, 1)
            for n in range(RING):
                split_hi(n)
            act.wait_ge(ns_ready, 1)
            root(D_MODEL, rs_ready)
            norm_hi(0)

            for j in range(4):
                split_hi(RING + j)
            take_hsum(0, 4)
            act.wait_ge(parm_in, 32)
            fn(dtp[0:HEADS, 2:3], dtp[0:HEADS, 1:2], ACTF.Exp).then_inc(dt_exp, 1)
            act.wait_ge(dt_in, 1)
            fn(dtw[0:HEADS, 2, :], dtw[0:HEADS, 1, :], ACTF.Exp).then_inc(dt_exp, 1)
            act.wait_ge(th_ready, 1)
            fn(s5p[:, 9, :], s5k[:, 0, :], ACTF.Sin, scale=TWO_PI).then_inc(sincos, 1)
            fn(s5p[:, 10, :], s5k[:, 0, :], ACTF.Sin, scale=TWO_PI / 2).then_inc(sincos, 1)

            turns, per, quads, u0, g0 = phase("u")
            with act.Fori(0, turns) as i:
                for r in range(per):
                    for j in range(quads):
                        split_hi(u0 + r * quads + j + RING, i * (per * quads))
                    take_hsum(g0 + r, u0 + (r + 1) * quads, i * per, i * (per * quads))

            def angles(tile):
                f = s5k[:, 0, ds(tile, 1)]
                step.begun(fn(ang[:, 0, :], iota[:, :], ACTF.Identity, scale=f))
                step.done(fn(ang[:, 1, :], iota[:, :], ACTF.Identity, scale=f, bias=0.25))
                fn(angm[:, :, :], ang[:, :, :], ACTF.Identity, bias=MAGIC).then_inc(angm_ready, 1)

            def group_hsum(name, i, r):
                _, per, quads, u0, g0 = phase(name)
                take_hsum(g0 + r, u0 + (r + 1) * quads, i * per, i * (per * quads))

            def group_silu(name, i, r):
                _, per, quads, u0, g0 = phase(name)
                if name == "zx" and r % 2 == 0:
                    act.wait_ge(sum_ready, i * per + (g0 + r + 1))
                    to = zx[:, ds(i * 4 + r, 2), 0, :]
                    fn(to, to, ACTF.Silu).then_inc(z_done, 1)
                elif name == "zx":
                    act.wait_ge(conv_done, i * 2 + (r // 2 + 1))
                    to = zx[:, ds(i * 4 + (r - 1), 2), 1, :]
                    fn(to, to, ACTF.Silu).then_inc(xbc_done, 1)
                else:
                    act.wait_ge(conv_done, i * per + (12 + r + 1))
                    to = bc[:, ds(i * 4 + r, 1), :, :].rearrange("p o c n -> p (o c) n")
                    fn(to, to, ACTF.Silu).then_inc(xbc_done, 1)

            def mixer_turn(name, i, blk, prev):
                _, per, quads, u0, g0 = phase(name)
                for r in range(per):
                    def hi(j):
                        split_hi(u0 + r * quads + j + RING, i * (per * quads))
                    before = (name, i, r - 1) if r else prev
                    last = name == "bc" and i == 1 and r == per - 1
                    if before:
                        group_hsum(*before)
                    hi(0)
                    if before:
                        act.wait_ge(x5_ready, blk * 4 + r)
                    act.wait_ge(ang_ready, blk * 4 + (r + 1))
                    fn(tab[:, :, :], ang[:, :, :], ACTF.Sin, scale=-TWO_PI).then_inc(tab_ready, 1)
                    hi(1)
                    if not last:
                        act.wait_ge(tab_ready, blk * 4 + (r + 1))
                        angles(blk * 4 + (r + 1))
                    hi(2)
                    if before:
                        group_silu(*before)
                    hi(3)

            act.wait_ge(iota_ready, 1)
            act.wait_ge(th_ready, 1)
            angles(0)
            mixer_turn("zx", 0, 0, None)
            with act.Fori(1, 6) as i:
                step.enter(i, 8, 1)
                mixer_turn("zx", i, i, ("zx", i - 1, 3))
                step.leave(6)
            mixer_turn("bc", 0, 6, ("zx", 5, 3))
            mixer_turn("bc", 1, 7, ("bc", 0, 3))
            group_hsum("bc", 1, 3)
            group_silu("bc", 1, 3)

            act.wait_ge(xbc_done, 20)
            act.wait_ge(z_done, 12)

            def group_root(g):
                act.wait_ge(yns_ready, g + 1)
                root(TPG * P, yrs_ready)

            def group_hi(g):
                act.wait_ge(yv_ready, g + 1)
                fn(y_hl[:, ds(g * TPG, TPG), 0:L], zx[:, ds(g * TPG, TPG), 1, :], ACTF.Copy).then_inc(yhi_ready, 1)

            def gate_turn(i, prev):
                _, per, quads, u0, g0 = phase("gate")

                def hi(j):
                    split_hi(u0 + j + RING, i * 8)

                def decay(half):
                    act.wait_ge(scan_ready, i * 2 + (half + 1))
                    fn(dec[half][:, :, :], dec[half][:, :, :], ACTF.Exp).then_inc(exp_ready, 1)

                fn(bst[:, :], bc[:, ds(i, 1), 0, :].rearrange("p o n -> p (o n)"), ACTF.Copy).then_inc(staged, 1)
                fn(xst[:, :, :], zx[:, ds(i * TPG, TPG), 1, :], ACTF.Copy).then_inc(staged, 1)
                hi(0)
                if prev is not None:
                    group_root(prev)
                hi(1)
                decay(0)
                hi(2)
                hi(3)
                decay(1)
                take_hsum(g0, u0 + 4, i * 2, i * 8)
                hi(4)
                if prev is not None:
                    group_hi(prev)
                hi(5)
                hi(6)
                hi(7)
                act.wait_ge(yz_ready, i + 1)
                fn(zx[:, ds(i * TPG, TPG), 0, :], zx[:, ds(i * TPG, TPG), 1, :], ACTF.Square).then_inc(ysq_ready, 1)
                take_hsum(g0 + 1, u0 + 8, i * 2, i * 8)

            gate_turn(0, None)
            with act.Fori(1, GROUPS) as i:
                step.enter(i, 1, 1)
                gate_turn(i, i - 1)
                step.leave(GROUPS)
            group_root(GROUPS - 1)
            group_hi(GROUPS - 1)

            act.wait_ge(y5_out, 8)
            fn(ub[:, :, :], ub[:, :, :], ACTF.Gelu_apprx_tanh).then_inc(y5_gelu, 1)
            act.wait_ge(y5_gelu, 1)
            act.wait_ge(ylo_ready, 8)
            fn(yb_hl[:, :, 0:L], ub[:, :, :], ACTF.Copy).then_inc(y5_hi, 1)
            act.wait_ge(sum_ready, GROUP0["proj"])

            turns, per, quads, u0, g0 = phase("proj")
            with act.Fori(0, turns) as i:
                for r in range(per):
                    to = gates[:, ds(i * 4 + 2 * r, 2), :]
                    fn(to, to, ACTF.Sigmoid).then_inc(ga_sig, 1)
                    for j in range(quads):
                        split_hi(u0 + r * quads + j + RING, i * (per * quads))
                    take_hsum(g0 + r, u0 + (r + 1) * quads, i * per, i * (per * quads))

            def glu_sigmoid(g):
                act.wait_ge(sum_ready, g + (GROUP0["glu"] + 1))
                fn(tsum[:, 1, :], tsum[:, 1, :], ACTF.Sigmoid).then_inc(glu_sig, 1)

            def merged_hi(g):
                act.wait_ge(m_sum, g + 1)
                fn(act16[:, ds(g, 1), 0:L], gates[:, ds(g, 1), :], ACTF.Copy).then_inc(m_hi, 1)

            def glu_turn(i, r, prev):
                _, per, quads, u0, g0 = phase("glu")
                to = gates[:, ds(i * 2 + (16 + r), 1), :]
                fn(to, to, ACTF.Sigmoid).then_inc(gb_sig, 1)
                split_hi(u0 + r * 2 + RING, i * 4)
                if prev is not None:
                    glu_sigmoid(prev)
                split_hi(u0 + r * 2 + 1 + RING, i * 4)
                if prev is not None:
                    merged_hi(prev)
                take_hsum(g0 + r, u0 + (r + 1) * 2, i * 2, i * 4)

            glu_turn(0, 0, None)
            glu_turn(0, 1, 0)
            with act.Fori(1, 8) as i:
                glu_turn(i, 0, i * 2 - 1)
                glu_turn(i, 1, i * 2)
            glu_sigmoid(15)
            merged_hi(15)

            def residual_phase(name, n, i, r, last=False):
                groups, quads, per = PHASES[name]
                u0, g0 = UNIT0[name], GROUP0[name]
                for j in range(quads):
                    if not (last and r == per - 1 and j >= quads - RING):
                        split_hi(u0 + r * quads + j + RING, i * (per * quads))
                take_hsum(g0 + r, u0 + (r + 1) * quads, i * per, i * (per * quads))
                act.wait_ge(sum_ready, i * per + (g0 + r + 1))
                act.wait_ge(sqacc_ready, i * per + (9 * n + r + 1))
                fn(sq[:, :, :], h[:, ds(i * (2 * per) + 2 * r, 2), :], ACTF.Square).then_inc(sq_ready, 1)

            with act.Fori(0, 4) as i:
                for r in range(2):
                    residual_phase("out", 0, i, r)
            act.wait_ge(ns_ready, 2)
            root(D_MODEL, rs_ready)
            norm_hi(1)

            def ff_silu(g):
                act.wait_ge(conv2_done, g + 1)
                fn(tsum[:, 0, :], tsum[:, 0, :], ACTF.Silu).then_inc(silu2_done, 1)

            def ff_hi(g):
                act.wait_ge(f_sum, g + 1)
                fn(ff[:, ds(g, 1), 0:L], tsum[:, 0:1, :], ACTF.Copy).then_inc(f_hi, 1)

            def up_turn(i, r, prev):
                _, per, quads, u0, g0 = phase("up")
                for j in range(4):
                    split_hi(u0 + r * 4 + j + RING, i * 8)
                    if prev is not None and j == 0:
                        ff_silu(prev)
                    if prev is not None and j == 2:
                        ff_hi(prev)
                take_hsum(g0 + r, u0 + (r + 1) * 4, i * 2, i * 8)

            up_turn(0, 0, None)
            up_turn(0, 1, 0)
            with act.Fori(1, 22) as i:
                up_turn(i, 0, i * 2 - 1)
                up_turn(i, 1, i * 2)
            ff_silu(43)
            ff_hi(43)

            for i in range(2):
                for r in range(4):
                    residual_phase("down", 1, i, r, last=i == 1)
            act.wait_ge(ns_ready, 3)
            root(D_MODEL, rs_ready)

        @block.vector
        def _(dve):
            step = Tally(dve, dve_step)
            V = nc.vector

            def split_lo(n, ahead=0):
                s = n % RING
                dve.wait_ge(hi_ready, ahead + (n + 1))
                V.tensor_tensor(wlo[:, s, :], raw[:, s, :], whi[:, s, :], ALU.subtract).then_inc(lo_ready, 1)

            def add_halves(to, g, gi=0):
                dve.wait_ge(hsum_ready, gi + (g + 1))
                tiles = slice(0, 2 if g else 1)
                V.tensor_tensor(to, sums(g, 0)[:, tiles, :], hsum[:, tiles, :], ALU.add).then_inc(sum_ready, 1)

            def norm_values(name, src, n, split=True):
                dve.wait_ge(rs_ready, n + 1)

                def lo(c):
                    dve.wait_ge(vhi_ready, 4 * n + c + 1)
                    k = slice(4 * c, 4 * c + 4)
                    V.tensor_tensor(act16[:, k, L:2 * L], vn[:, k, :], act16[:, k, 0:L],
                                    ALU.subtract).then_inc(vlo_ready, 1)
                for c in range(4):
                    for k in range(4 * c, 4 * c + 4):
                        ins = V.scalar_tensor_tensor(vn[:, k, :], src[:, k, :], col(name, k), rs[:, :],
                                                     ALU.mult, ALU.mult)
                    ins.then_inc(v_ready, 1)
                    if split and c:
                        lo(c - 1)
                if split:
                    lo(3)

            def horner(to, x, coefs):
                step.done(V.tensor_scalar(to, x, coefs[0], None, ALU.mult))
                for c in coefs[1:]:
                    step.done(V.scalar_tensor_tensor(to, to, c, x, ALU.add, ALU.mult))

            def mul(to, x, y, op=ALU.mult):
                step.done(V.tensor_tensor(to, x, y, op))

            for n in range(RING):
                split_lo(n)
            dve.wait_ge(parm_in, 32)
            norm_values("norm_mix", xin, 0)

            for j in range(4):
                split_lo(RING + j)
            add_halves(tsum[:, 0:1, :], 0)
            dve.wait_ge(sum_ready, 1)
            d = [dtw[0:HEADS, k, :] for k in range(7)]
            step.done(V.tensor_scalar(d[0], tsum[0:HEADS, 0, :], dtp[0:HEADS, 0:1], None, ALU.add))
            V.scalar_tensor_tensor(d[1], d[0], -1.0, d[0], ALU.mult, ALU.min).then_inc(dt_in, 1)
            dve.wait_ge(dt_exp, 2)
            step.done(V.tensor_scalar(d[3], d[2], 2.0, None, ALU.add))
            step.done(V.reciprocal(d[3], d[3]))
            mul(d[3], d[3], d[2])
            mul(d[4], d[3], d[3])
            horner(d[5], d[4], [1.0 / k for k in (13, 11, 9, 7, 5, 3)])
            step.done(V.scalar_tensor_tensor(d[5], d[5], 1.0, d[3], ALU.add, ALU.mult))
            step.done(V.tensor_scalar(d[0], d[0], 0.0, None, ALU.max))
            step.done(V.scalar_tensor_tensor(d[6], d[5], 2.0, d[0], ALU.mult, ALU.add))
            V.tensor_scalar(d[5], d[6], dtp[0:HEADS, 2:3], -1.0, ALU.mult, ALU.mult).then_inc(dt_row, 1)

            s = [s5p[:, k, :] for k in range(20)]
            lam_im, angle, modulus = s5in[:, 1, :], s5k[:, 0, :], s5k[:, 1, :]
            dve.wait_ge(s5_in, 32)
            dve.wait_ge(const_ready, 9)
            V.tensor_copy(iota[:, :], iotai[:, :]).then_inc(iota_ready, 1)
            step.done(V.tensor_scalar(s[0], s5in[:, 0, :], EIG_MAX, None, ALU.min))
            step.done(V.tensor_scalar(s[1], s5in[:, 2, :], -87.0, 88.0, ALU.max, ALU.min))
            step.done(V.tensor_scalar(s[2], s[1], LOG2E, MAGIC, ALU.mult, ALU.add))
            step.done(V.tensor_scalar(s[2], s[2], MAGIC, None, ALU.subtract))
            step.done(V.scalar_tensor_tensor(s[1], s[2], -LN2_HI, s[1], ALU.mult, ALU.add))
            step.done(V.scalar_tensor_tensor(s[1], s[2], -LN2_LO, s[1], ALU.mult, ALU.add))
            horner(s[3], s[1], [1.0 / math.factorial(k) for k in range(7, 0, -1)])
            step.done(V.tensor_scalar(s5i[:, :], s[2], 127.0, 8388608.0, ALU.add, ALU.mult))
            step.done(V.scalar_tensor_tensor(s[4], s[3], 1.0, s5i[:, :].bitcast(F32), ALU.add, ALU.mult))
            mul(s[6], lam_im, s[4])
            step.done(V.tensor_scalar(s[6], s[6], 1.0 / (2 * math.pi), None, ALU.mult))
            step.done(V.tensor_scalar(s[7], s[6], MAGIC, None, ALU.add))
            step.done(V.tensor_scalar(s[7], s[7], MAGIC, None, ALU.subtract))
            mul(s[6], s[6], s[7], ALU.subtract)
            V.tensor_scalar(angle, s[6], 0.5, -0.5, ALU.min, ALU.max).then_inc(th_ready, 1)
            mul(s[5], s[0], s[4])
            step.done(V.tensor_scalar(s[5], s[5], -88.0, 1.0 / 256, ALU.max, ALU.mult))
            horner(s[8], s[5], [1.0 / math.factorial(k) for k in range(6, 0, -1)])
            for _ in range(8):
                step.done(V.scalar_tensor_tensor(s[8], s[8], 2.0, s[8], ALU.add, ALU.mult))
            step.done(V.tensor_scalar(modulus, s[8], 1.0, None, ALU.add))
            dve.wait_ge(sincos, 2)
            step.done(V.scalar_tensor_tensor(s[11], s[10], 2.0, s[10], ALU.mult, ALU.mult))
            mul(s[12], modulus, s[11])
            mul(s[12], s[8], s[12], ALU.subtract)
            mul(s[13], modulus, s[9])
            mul(s[14], s[0], s[0])
            mul(s[15], lam_im, lam_im)
            mul(s[14], s[14], s[15], ALU.add)
            step.done(V.reciprocal(s[15], s[14]))
            mul(s[16], s[12], s[0])
            mul(s[17], s[13], lam_im)
            mul(s[16], s[16], s[17], ALU.add)
            mul(s[16], s[16], s[15])
            mul(s[18], s[13], s[0])
            mul(s[19], s[12], lam_im)
            mul(s[18], s[18], s[19], ALU.subtract)
            mul(s[18], s[18], s[15])
            def wide(k):
                return s5p[:, k:k + 1, :].rearrange("p o j -> p j o").to_broadcast([P, S5T, 16])
            cr, ci, t0, t1 = craw[:, 0], craw[:, 1], ctmp[:, 0], ctmp[:, 1]
            mul(t0, cr, wide(16))
            mul(t1, ci, wide(18))
            mul(cfold[:, 0], t0, t1, ALU.subtract)
            mul(t0, cr, wide(18))
            mul(t1, ci, wide(16))
            step.done(V.scalar_tensor_tensor(cfold[:, 1], t0, -1.0, t1, ALU.mult, ALU.subtract))

            def phase(name):
                groups, quads, per = PHASES[name]
                return groups // per, per, quads, UNIT0[name], GROUP0[name]

            turns, per, quads, u0, g0 = phase("u")
            with dve.Fori(0, turns) as i:
                for r in range(per):
                    for j in range(quads):
                        split_lo(u0 + r * quads + j + RING, i * (per * quads))
                    add_halves(ub[:, ds(i * 4 + 2 * r, 2), :], g0 + r, i * per)
            dve.wait_ge(dt_T, 1)
            V.tensor_copy(dtt[:, :, :], DTT).then_inc(dt_v, 1)

            sin2, cos2 = (tab[:, k:k + 1, :].to_broadcast([P, 2, L]) for k in range(2))

            def s5_fractions(count):
                dve.wait_ge(angm_ready, count)
                V.scalar_tensor_tensor(ang[:, :, :], angm[:, :, :], MAGIC, ang[:, :, :], ALU.subtract,
                                       ALU.subtract).then_inc(ang_ready, 1)

            def s5_scan(r, tile, count, first=False):
                if not first:
                    dve.wait_ge(y5_ready, tile)
                dve.wait_ge(tab_ready, count)
                dve.wait_ge(bu_ready, count)
                step.begun(V.tensor_tensor(rot1[:, :, :], BU[r % 2], cos2, ALU.mult))
                mul(rot2[:, :, :], BU[r % 2], sin2)
                step.begun(V.tensor_tensor(st[:, 0, :], rot1[:, 0, :], rot2[:, 1, :], ALU.add))
                mul(st[:, 1, :], rot1[:, 1, :], rot2[:, 0, :], ALU.subtract)
                m = s5k[:, 1, ds(tile, 1)].to_broadcast([P, L])
                step.begun(V.tensor_tensor_scan(rot1[:, 0, :], m, st[:, 0, :], 0.0, ALU.mult, ALU.add))
                step.done(V.tensor_tensor_scan(rot1[:, 1, :], m, st[:, 1, :], 0.0, ALU.mult, ALU.add))

            def s5_states():
                step.begun(V.tensor_tensor(rot2[:, :, :], rot1[:, :, :], cos2, ALU.mult))
                mul(rot3[:, :, :], rot1[:, :, :], sin2)
                V.tensor_tensor(st[:, 0, :], rot2[:, 0, :], rot3[:, 1, :], ALU.subtract)
                V.tensor_tensor(st[:, 1, :], rot2[:, 1, :], rot3[:, 0, :], ALU.add).then_inc(x5_ready, 1)

            def conv_pair(to, tile, taps, w, b, ready):
                for k in range(taps - 1, -1, -1):
                    off = 3 - (taps - 1) + k
                    for t in range(2):
                        src, q = cpad[:, t, off:off + L], tile + t
                        if k == taps - 1:
                            ins = V.tensor_scalar(to[t], src, col(w, q * taps + k), col(b, q), ALU.mult, ALU.add)
                        else:
                            step.hold(but=1)
                            ins = V.scalar_tensor_tensor(to[t], src, col(w, q * taps + k), to[t], ALU.mult, ALU.add)
                        if k or not t:
                            step.begun(ins)
                ins.then_inc(ready, 1)

            def s5_out(blk):
                dve.wait_ge(y5_ready, blk * 4 + 4)
                to = ub[:, ds(blk, 1), :].rearrange("p o n -> p (o n)")
                V.scalar_tensor_tensor(to, to, col("s5_d", blk), YS5, ALU.mult, ALU.add).then_inc(y5_out, 1)

            def group_end(name, i, r):
                _, per, quads, u0, g0 = phase(name)
                if name == "zx" and r % 2 == 0:
                    add_halves(zx[:, ds(i * 4 + r, 2), 0, :], g0 + r, i * per)
                    return
                add_halves(cpad[:, :, 3:3 + L], g0 + r, i * per)
                dve.wait_ge(sum_ready, i * per + (g0 + r + 1))
                if name == "zx":
                    to = [zx[:, ds(i * 4 + (r - 1 + t), 1), 1, :].rearrange("p o n -> p (o n)") for t in range(2)]
                    conv_pair(to, i * 4 + (r - 1), 4, "conv_a_w", "conv_a_b", conv_done)
                else:
                    to = [bc[:, ds(i * 4 + r, 1), t, :].rearrange("p o n -> p (o n)") for t in range(2)]
                    conv_pair(to, i * 8 + (24 + 2 * r), 4, "conv_a_w", "conv_a_b", conv_done)

            def cpad_free(name, i, r):
                if name == "bc":
                    dve.wait_ge(conv_done, i * 4 + (12 + r + 1))
                elif r % 2:
                    dve.wait_ge(conv_done, i * 2 + (r // 2 + 1))

            def mixer_turn(name, i, blk, prev):
                _, per, quads, u0, g0 = phase(name)
                for r in range(per):
                    def lo(j):
                        split_lo(u0 + r * quads + j + RING, i * (per * quads))
                    before = (name, i, r - 1) if r else prev
                    last = name == "bc" and i == 1 and r == per - 1
                    lo(0)
                    if before:
                        group_end(*before)
                    lo(1)
                    if before:
                        cpad_free(*before)
                    s5_scan(r, blk * 4 + r, blk * 4 + (r + 1), not before)
                    lo(2)
                    if r == 0:
                        if prev:
                            s5_out(blk - 1)
                        for g in range(2):
                            rows = slice(64 * g, 64 * g + 64)
                            ins = V.tensor_copy(cz[rows, :, :, 16 * g:16 * g + 16],
                                                cfold[rows, :, ds(blk * 4, 4), :].rearrange("p c r n -> p r c n"))
                        ins.then_inc(cz_ready, 1)
                    s5_states()
                    if not last:
                        s5_fractions(blk * 4 + (r + 2))
                    lo(3)

            s5_fractions(1)
            mixer_turn("zx", 0, 0, None)
            with dve.Fori(1, 6) as i:
                step.enter(i, 4 * 8 + 2 * 7, 1)
                mixer_turn("zx", i, i, ("zx", i - 1, 3))
                step.leave(6)
            mixer_turn("bc", 0, 6, ("zx", 5, 3))
            mixer_turn("bc", 1, 7, ("bc", 0, 3))
            group_end("bc", 1, 3)
            cpad_free("bc", 1, 3)
            s5_out(7)

            dve.wait_ge(z_done, 12)
            dve.wait_ge(xbc_done, 20)

            def group_norm(g):
                dve.wait_ge(yrs_ready, g + 1)
                for k in range(TPG):
                    x = zx[:, ds(g * TPG + k, 1), 1, :].rearrange("p o n -> p (o n)")
                    ins = V.scalar_tensor_tensor(x, x, col("norm_a", g * TPG + k), rs[:, :], ALU.mult, ALU.mult)
                ins.then_inc(yv_ready, 1)

            def group_lo(g):
                q = ds(g * TPG, TPG)
                dve.wait_ge(yhi_ready, g + 1)
                V.tensor_tensor(y_hl[:, q, L:2 * L], zx[:, q, 1, :], y_hl[:, q, 0:L],
                                ALU.subtract).then_inc(ylo_ready, 1)

            def gate_turn(i, prev):
                _, per, quads, u0, g0 = phase("gate")

                def lo(j):
                    split_lo(u0 + j + RING, i * 8)

                def scan(half):
                    dve.wait_ge(dec_in[half], i * 32 + 32)
                    for k in range(HALF):
                        ins = V.tensor_tensor_scan(dec[half][:, k, :], dec[half][:, k, :], mask[:, :], 0.0,
                                                   ALU.add, ALU.mult)
                    ins.then_inc(scan_ready, 1)

                def blocks(half):
                    dve.wait_ge(exp_ready, i * 2 + (half + 1))
                    V.tensor_tensor(dec[half][:, :, :], dec[half][:, :, :],
                                    cbm[:, :].rearrange("p (o n) -> p o n", o=1).to_broadcast([P, HALF, ML]),
                                    ALU.mult).then_inc(m_ready, 1)

                lo(0)
                scan(0)
                lo(1)
                dve.wait_ge(cb_ready, i + 1)
                V.tensor_tensor(cbm[:, :], CB, mask_in[:, :], ALU.mult)
                dve.wait_ge(xp_ready, i + 1)
                for k in range(2):
                    ins = V.tensor_tensor(
                        xtok[:, k, :].rearrange("p (h n) -> p h n", h=HPG), XP[k].rearrange("p (h n) -> p h n", h=HPG),
                        dtt[:, k, ds(i * HPG, HPG)].rearrange("p (h o) -> p h o", o=1).to_broadcast([P, HPG, 64]),
                        ALU.mult)
                step.done(ins)
                lo(2)
                scan(1)
                if prev is not None:
                    group_norm(prev)
                lo(3)
                blocks(0)
                add_halves(gates[:, ds(i * 4, 2), :], g0, i * 2)
                lo(4)
                blocks(1)
                lo(5)
                if prev is not None:
                    group_lo(prev)
                lo(6)
                dve.wait_ge(y_ready, i * 2 + 2)
                for k in range(TPG):
                    x = zx[:, ds(i * TPG + k, 1), 1, :].rearrange("p o n -> p (o n)")
                    ins = V.scalar_tensor_tensor(x, x, col("d_a", i * TPG + k), YY[k], ALU.mult, ALU.add)
                step.done(ins)
                q = ds(i * TPG, TPG)
                V.tensor_tensor(zx[:, q, 1, :], zx[:, q, 1, :], zx[:, q, 0, :], ALU.mult).then_inc(yz_ready, 1)
                lo(7)
                add_halves(gates[:, ds(i * 4 + 2, 2), :], g0 + 1, i * 2)

            gate_turn(0, None)
            with dve.Fori(1, GROUPS) as i:
                step.enter(i, 2, 1)
                gate_turn(i, i - 1)
                step.leave(GROUPS)
            group_norm(GROUPS - 1)
            group_lo(GROUPS - 1)

            dve.wait_ge(y5_hi, 1)
            V.tensor_tensor(yb_hl[:, :, L:2 * L], ub[:, :, :], yb_hl[:, :, 0:L], ALU.subtract).then_inc(y5_lo, 1)

            turns, per, quads, u0, g0 = phase("proj")
            with dve.Fori(0, turns) as i:
                step.enter(i, 2)
                for r in range(per):
                    for j in range(quads):
                        split_lo(u0 + r * quads + j + RING, i * (per * quads))
                    add_halves(tsum[:, :, :], g0 + r, i * per)
                    dve.wait_ge(sum_ready, i * per + (g0 + r + 1))
                    dve.wait_ge(ga_sig, i * per + (r + 1))
                    to = gates[:, ds(i * 4 + 2 * r, 2), :]
                    mul(to, tsum[:, :, :], to)
                step.leave(turns)

            def merge(g):
                gb, ga = gates[:, ds(g + 16, 1), :], gates[:, ds(g, 1), :]
                dve.wait_ge(glu_sig, g + 1)
                mul(tsum[:, 0, :], tsum[:, 0, :], tsum[:, 1, :])
                mul(tsum[:, 0:1, :], tsum[:, 0:1, :], gb)
                V.tensor_tensor(ga, ga, tsum[:, 0:1, :], ALU.add).then_inc(m_sum, 1)

            def merged_lo(g):
                dve.wait_ge(m_hi, g + 1)
                to = act16[:, ds(g, 1), :]
                V.tensor_tensor(to[:, :, L:2 * L], gates[:, ds(g, 1), :], to[:, :, 0:L], ALU.subtract).then_inc(m_lo, 1)

            def glu_turn(i, r, prev):
                _, per, quads, u0, g0 = phase("glu")
                split_lo(u0 + r * 2 + RING, i * 4)
                if prev is not None:
                    merge(prev)
                split_lo(u0 + r * 2 + 1 + RING, i * 4)
                if prev is not None:
                    merged_lo(prev)
                add_halves(tsum[:, :, :], g0 + r, i * 2)

            glu_turn(0, 0, None)
            glu_turn(0, 1, 0)
            with dve.Fori(1, 8) as i:
                step.enter(i, 4, 1)
                glu_turn(i, 0, i * 2 - 1)
                glu_turn(i, 1, i * 2)
                step.leave(8)
            merge(15)
            merged_lo(15)

            def residual_phase(name, i, r, last=False):
                groups, quads, per = PHASES[name]
                u0, g0 = UNIT0[name], GROUP0[name]
                for j in range(quads):
                    if not (last and r == per - 1 and j >= quads - RING):
                        split_lo(u0 + r * quads + j + RING, i * (per * quads))
                hg = h[:, ds(i * (2 * per) + 2 * r, 2), :]
                dve.wait_ge(h_in, 16)
                dve.wait_ge(hsum_ready, i * per + (g0 + r + 1))
                mul(hg, hg, hsum[:, :, :], ALU.add)
                V.tensor_tensor(hg, sums(g0 + r, 0), hg, ALU.add).then_inc(sum_ready, 1)

            with dve.Fori(0, 4) as i:
                step.enter(i, 2)
                for r in range(2):
                    residual_phase("out", i, r)
                step.leave(4)
            dve.wait_ge(sum_ready, GROUP0["up"])
            norm_values("norm_ffn", h, 1)

            def ff_product(g):
                dve.wait_ge(silu2_done, g + 1)
                V.tensor_tensor(tsum[:, 0, :], tsum[:, 0, :], tsum[:, 1, :], ALU.mult).then_inc(f_sum, 1)

            def ff_lo(g):
                dve.wait_ge(f_hi, g + 1)
                to = ff[:, ds(g, 1), :]
                V.tensor_tensor(to[:, :, L:2 * L], tsum[:, 0:1, :], to[:, :, 0:L], ALU.subtract).then_inc(f_lo, 1)
                dve.wait_ge(f_lo, g + 1)

            def up_turn(i, r, prev):
                _, per, quads, u0, g0 = phase("up")
                for j in range(4):
                    split_lo(u0 + r * 4 + j + RING, i * 8)
                    if prev is not None and j == 1:
                        ff_product(prev)
                    if prev is not None and j == 3:
                        ff_lo(prev)
                add_halves(cpad[:, :, 3:3 + L], g0 + r, i * 2)
                dve.wait_ge(sum_ready, i * 2 + (g0 + r + 1))
                conv_pair([tsum[:, t, :] for t in range(2)], i * 4 + 2 * r, 3, "conv_f_w", "conv_f_b", conv2_done)

            up_turn(0, 0, None)
            up_turn(0, 1, 0)
            with dve.Fori(1, 22) as i:
                step.enter(i, 10, 1)
                up_turn(i, 0, i * 2 - 1)
                up_turn(i, 1, i * 2)
                step.leave(22)
            ff_product(43)
            ff_lo(43)

            for i in range(2):
                for r in range(4):
                    residual_phase("down", i, r, last=i == 1)
            dve.wait_ge(sum_ready, N_ALL)
            norm_values("norm_final", h, 2, split=False)

        @block.tensor
        def _(pe):
            mm = nc.tensor.matmul

            def unit(name, r, q, act, i=0):
                groups, quads, per = PHASES[name]
                n, g = UNIT0[name] + r * quads + q, GROUP0[name] + r
                pe.wait_ge(lo_ready, i * (per * quads) + (n + 1))
                if q == 0 and g >= 1:
                    pe.wait_ge(sum_ready, i * per + (g - 1 if g >= 2 else g))
                s, b = n % RING, 2 * (g % 2)
                for k in range(4):
                    x = act[:, 4 * q + k, :]
                    first, last = q == 0 and k == 0, q == quads - 1 and k == 3
                    for t in range(1 if name == "dt" else 2):
                        cols = slice(k * L + t * P, k * L + t * P + P)
                        mm(psum[:, b + t, :], whi[:, s, cols], x, start=first, stop=False)
                        ins = mm(psum[:, b + t, L:2 * L], wlo[:, s, cols], x[:, 0:L], start=False, stop=last)
                ins.then_inc(unit_used, 1)

            def ones_sum(parts):
                for k, x in enumerate(parts):
                    ins = mm(NS, ones[:, :], x, start=k == 0, stop=k == len(parts) - 1)
                return ins

            pe.wait_ge(const_ready, 1)
            for k in range(KT):
                if k % 4 == 0:
                    pe.wait_ge(xsq_ready, k // 4 + 1)
                ins = mm(NS, ones[:, :], xsq[:, k, :], start=k == 0, stop=k == KT - 1)
            ins.then_inc(ns_ready, 1)

            for q in range(4):
                pe.wait_ge(vlo_ready, q + 1)
                unit("dt", 0, q, act16)
            with pe.Fori(0, 2) as i:
                for r in range(2):
                    for q in range(4):
                        unit("u", r, q, act16, i)
            pe.wait_ge(const_ready, 9)
            pe.wait_ge(dt_row, 1)
            for k in range(2):
                ins = nc.tensor.transpose(DTT[:, k, :], dtw[0:HEADS, 6, k * P:k * P + P], ident[0:HEADS, 0:HEADS])
            ins.then_inc(dt_T, 1)
            pe.wait_ge(sum_ready, GROUP0["zx"])
            def s5_product(r, tile):
                pe.wait_ge(x5_ready, tile + 1)
                for k in range(2):
                    ins = mm(YS5[32 * r:32 * r + 32], cz[:, r, k, :], st[:, k, :], start=k == 0, stop=k == 1)
                ins.then_inc(y5_ready, 1)

            def mixer_turn(name, i, blk, prev):
                for r in range(4):
                    pe.wait_ge(b_in[r], blk * 32 + 32)
                    for k in range(2):
                        ins = mm(BU[r % 2][:, k, :], bz[:, r, k, :],
                                 ub[:, ds(blk, 1), :].rearrange("p o n -> p (o n)"), start=True, stop=True)
                    ins.then_inc(bu_ready, 1)
                    unit(name, r, 0, act16, i)
                    unit(name, r, 1, act16, i)
                    if r:
                        if r == 1:
                            pe.wait_ge(cz_ready, blk + 1)
                        s5_product(r - 1, blk * 4 + (r - 1))
                    elif prev is not None:
                        s5_product(3, prev * 4 + 3)
                    for q in range(2, 4):
                        unit(name, r, q, act16, i)

            mixer_turn("zx", 0, 0, None)
            with pe.Fori(1, 6) as i:
                mixer_turn("zx", i, i, i - 1)
            with pe.Fori(0, 2) as i:
                mixer_turn("bc", i, i + 6, i + 5)
            s5_product(3, 31)

            def group_squares(g):
                pe.wait_ge(ysq_ready, g + 1)
                ones_sum([zx[:, ds(g * TPG + t, 1), 0, :].rearrange("p o n -> p (o n)")
                          for t in range(TPG)]).then_inc(yns_ready, 1)

            def gate_turn(i, prev):
                def heads(half):
                    pe.wait_ge(m_ready, i * 2 + (half + 1))
                    for k in range(HALF):
                        hd = half * HALF + k
                        y = YY[hd // 2][64 * (hd % 2):64 * (hd % 2) + 64]
                        x = slice(64 * hd, 64 * hd + 64)
                        mm(y, xtok[:, 0, x], dec[half][:, k, 0:L], start=True, stop=False)
                        ins = mm(y[:, P:L], xtok[:, 1, x], dec[half][:, k, L:ML], start=False, stop=True)
                    ins.then_inc(y_ready, 1)

                unit("gate", 0, 0, act16, i)
                if prev is not None:
                    group_squares(prev)
                pe.wait_ge(staged, i * 2 + 2)
                c = bc[:, ds(i, 1), 1, :].rearrange("p o n -> p (o n)")
                mm(CB[:, 0:L], bst[:, 0:P], c, start=True, stop=True)
                mm(CB[:, L:ML], bst[:, P:L], c[:, P:L], start=True, stop=True).then_inc(cb_ready, 1)
                for k in range(2):
                    for t in range(TPG):
                        ins = nc.tensor.transpose(XP[k][:, t * P:t * P + P], xst[:, t, k * P:k * P + P], ident[:, :])
                ins.then_inc(xp_ready, 1)
                for q in range(1, 4):
                    unit("gate", 0, q, act16, i)
                unit("gate", 1, 0, act16, i)
                heads(0)
                unit("gate", 1, 1, act16, i)
                heads(1)
                unit("gate", 1, 2, act16, i)
                unit("gate", 1, 3, act16, i)

            pe.wait_ge(y5_out, 8)
            gate_turn(0, None)
            with pe.Fori(1, GROUPS) as i:
                gate_turn(i, i - 1)
            group_squares(GROUPS - 1)

            for name, src, ready in (("proj", y_hl, ylo_ready), ("glu", yb_hl, y5_lo), ("out", act16, m_lo),
                                     ("up", act16, vlo_ready), ("down", ff, f_lo)):
                groups, quads, per = PHASES[name]
                if name == "up":
                    pe.wait_ge(sqacc_ready, 9)
                    ones_sum([sqacc[:, k, :] for k in range(2)]).then_inc(ns_ready, 1)
                with pe.Fori(0, groups // per) as i:
                    for r in range(per):
                        for q in range(quads):
                            if r == 0:
                                pe.wait_ge(ready, {"proj": (4 * q + 3) // TPG + 1, "glu": 1, "up": 4 + q + 1,
                                                   }.get(name, 4 * q + 4))
                            unit(name, r, q, src, i)
            pe.wait_ge(sqacc_ready, 18)
            ones_sum([sqacc[:, k, :] for k in range(2)]).then_inc(ns_ready, 1)

    return nc


def _units(w):
    rows, cols = w.shape
    w = w.reshape(rows // 512, 4, P, cols // 256, 256).transpose(3, 0, 2, 1, 4)
    return np.ascontiguousarray(w).reshape(-1, P, UNIT)


def _pairs(x, y, width=P):
    lead = x.shape[:-1]
    x, y = x.reshape(*lead, -1, 1, width), y.reshape(*lead, -1, 1, width)
    return np.concatenate([x, y], axis=-2).reshape(*lead, -1)


def _tiles(v):
    return v.reshape(-1, P).T


def _conv(w):
    return w.reshape(w.shape[0], -1, P).transpose(2, 1, 0).reshape(P, -1)


def kernel(**inputs):
    import concourse.bacc as bacc
    from concourse.bass_utils import run_bass_kernel_spmd

    v = {k: np.asarray(x) for k, x in inputs.items()}
    w_in = v["w_in"][0]
    cut = np.cumsum([0, D_INNER, D_INNER, 1024, 1024, HEADS, D_S5, 2 * D_MODEL])
    z, x, b, c, dt, u, gate = (w_in[:, cut[k]:cut[k + 1]] for k in range(7))
    glu, up = v["w_s5_glu"][0], v["w_up"][0]
    cw, cb, fw, fb = v["conv_a_w"][0], v["conv_a_b"][0], v["conv_ffn_w"][0], v["conv_ffn_b"][0]

    def xbc_order(m):
        return np.concatenate([m[..., :D_INNER], _pairs(m[..., D_INNER:D_INNER + 1024], m[..., D_INNER + 1024:])], axis=-1)

    def halves(m):
        n = m.shape[-1] // 2
        return _pairs(m[..., :n], m[..., n:])

    a = {
        "x": np.ascontiguousarray(v["x"][0].reshape(L, KT, P).transpose(2, 1, 0)),
        "w_dt": _units(w_in[:, cut[4]:cut[4] + 256]), "w_u": _units(u), "w_zx": _units(_pairs(z, x, 256)),
        "w_bc": _units(_pairs(b, c)), "w_gate": _units(gate), "w_proj": _units(v["w_proj_a"][0]),
        "w_glu": _units(halves(glu)), "w_out": _units(v["w_out"][0]), "w_up": _units(halves(up)),
        "w_down": _units(v["w_down"][0]),
        "dtp": np.ascontiguousarray(np.stack([v["dt_bias"][0], v["a_log"][0]], axis=1)),
        "s5_lam": np.ascontiguousarray(np.stack(
            [v["s5_lam_re"][0], v["s5_lam_im"][0],
             np.broadcast_to(v["s5_log_dt"][0][:, None], (64, 64))]).reshape(3, S5T, P).transpose(2, 0, 1)),
        "s5_c": np.ascontiguousarray(np.stack([v["s5_c_re"][0], v["s5_c_im"][0]])
                                     .transpose(0, 1, 3, 2).reshape(2, S5T, P, 16).transpose(2, 0, 1, 3)),
        "s5_b": np.ascontiguousarray(np.stack([v["s5_b_re"][0], v["s5_b_im"][0]]).transpose(1, 3, 0, 2)),
    }
    a["parm"] = np.ascontiguousarray(np.concatenate([
        _tiles(v["norm_mix_w"][0]), _tiles(v["norm_ffn_w"][0]), _tiles(v["norm_final_w"]), _tiles(v["norm_a_w"][0]),
        _tiles(np.repeat(v["d_a"][0], 64)), _conv(xbc_order(cw)), _tiles(xbc_order(cb)), _conv(halves(fw)),
        _tiles(halves(fb)), _tiles(v["s5_d"][0])], axis=1))

    nc = bacc.Bacc("TRN2", target_bir_lowering=False, num_devices=1)
    aps = {k: nc.dram_tensor(f"in_{k}", m.shape, mybir.dt.from_np(m.dtype), kind="ExternalInput").ap()
           for k, m in a.items()}
    out = nc.dram_tensor("out", (P, KT, L), F32, kind="ExternalOutput").ap()
    build_program(nc, aps, out)
    r = run_bass_kernel_spmd(nc, [{f"in_{k}": m for k, m in a.items()}], core_ids=[0])
    y = r.results[0]["out"]
    return np.ascontiguousarray(y.transpose(2, 1, 0)).reshape(1, L, D_MODEL)
```

```python
import math
from contextlib import ExitStack

import numpy as np
import concourse.bass as bass
from concourse import mybir

F32, F32R, I32 = mybir.dt.float32, mybir.dt.float32r, mybir.dt.int32
ALU, ACTF = mybir.AluOpType, mybir.ActivationFunctionType
ds = bass.ds

P = 128
L = 256
D_MODEL, D_INNER, D_S5, D_FF = 2048, 3072, 1024, 5632
HEADS, GROUPS = 48, 8
HPG = HEADS // GROUPS
HALF = HPG // 2
TPG = D_INNER // GROUPS // P
EPS, EIG_MAX = 1e-6, -1e-4
KT = D_MODEL // P
S5T = 32
RING = 4
UNIT = 4 * 256
ML = L + P

PHASES = {"dt": (1, 4, 1), "u": (4, 4, 2), "zx": (24, 4, 4), "bc": (8, 4, 4), "gate": (16, 4, 2),
          "proj": (8, 6, 2), "glu": (16, 2, 2), "out": (8, 4, 2), "up": (44, 4, 2), "down": (8, 11, 4)}
UNIT0, GROUP0, N_UNITS, N_ALL = {}, {}, 0, 0
for _n, (_g, _q, _b) in PHASES.items():
    UNIT0[_n], GROUP0[_n] = N_UNITS, N_ALL
    N_UNITS, N_ALL = N_UNITS + _g * _q, N_ALL + _g

PARM = {}
_at = 0
for _n, _w in (("norm_mix", 16), ("norm_ffn", 16), ("norm_final", 16), ("norm_a", 24), ("d_a", 24),
               ("conv_a_w", 160), ("conv_a_b", 40), ("conv_f_w", 264), ("conv_f_b", 88), ("s5_d", 8)):
    PARM[_n] = _at
    _at += _w
N_PARM = _at

LOG2E, LN2_HI, LN2_LO = 1.4426950408889634, 0.693359375, -2.12194440054690583e-4
MAGIC = 12582912.0
TWO_PI = 6.2831850


class Tally:

    def __init__(self, eng, sem):
        self.eng, self.sem, self.n, self.i, self.per, self.start = eng, sem, 0, None, 0, 0

    def enter(self, i, per, first=0):
        self.i, self.per, self.first, self.start = i, per, first, self.n

    def leave(self, turns):
        assert self.n - self.start == self.per, f"{self.n - self.start} steps in a turn, not {self.per}"
        self.i, self.n = None, self.start + (turns - self.first) * self.per

    def begun(self, ins):
        ins.then_inc(self.sem, 1)
        self.n += 1

    def hold(self, but=0):
        n = self.n - but
        self.eng.wait_ge(self.sem, n if self.i is None else self.i * self.per + (n - self.first * self.per))

    def done(self, ins):
        self.begun(ins)
        self.hold()


def build_program(nc, a, out):
    ctx = ExitStack()
    with ctx:
        base = nc.sbuf_base + -nc.sbuf_base % 64
        room = nc.sbuf_usable_end - base
        K = 1024

        def at(name, shape, dt, off):
            size = 4 * math.prod(shape[1:])
            assert off + size <= room, (name, off, size, room)
            return nc.alloc_sbuf_tensor_at(name, shape, dt, offset=base + off)

        raw = at("raw", [P, RING, UNIT], F32, 0)
        whi = at("whi", [P, RING, UNIT], F32R, 16 * K)
        wlo = at("wlo", [P, RING, UNIT], F32R, 32 * K)
        act16 = at("act16", [P, KT, 2 * L], F32R, 48 * K)
        zx = at("zx", [P, 24, 2, L], F32, 80 * K)
        y_hl = at("y_hl", [P, 24, 2 * L], F32R, 80 * K)
        vn = at("vn", [P, KT, L], F32, 80 * K)
        nw = at("nw", [P, KT, 2 * L], F32R, 80 * K)
        ff = at("ff", [P, 60, 2 * L], F32R, 48 * K)
        gates = at("gates", [P, 32, L], F32, 128 * K)
        bc = at("bc", [P, GROUPS, 2, L], F32, 152 * K)
        xin = at("xin", [P, KT, L], F32, 152 * K)
        ub = at("ub", [P, 8, L], F32, 168 * K)
        h = at("h", [P, KT, L], F32, 168 * K)
        yb_hl = at("yb_hl", [P, 8, 2 * L], F32R, 181 * K)
        tab = [at("tab0", [P, 2, L], F32, 128 * K), at("tab1", [P, 2, L], F32, 150 * K)]
        ang = at("ang", [P, 2, L], F32, 130 * K)
        rot1 = at("rot1", [P, 2, L], F32, 132 * K)
        rot2 = at("rot2", [P, 2, L], F32, 134 * K)
        st = [at("st0", [P, 2, L], F32, 185 * K + 256), at("st1", [P, 2, L], F32, 136 * K)]
        bz = at("bz", [P, 4, 2, P], F32, 138 * K)
        cz = at("cz", [P, 4, 2, 32], F32, 142 * K)
        cfold = at("cfold", [P, 2, S5T, 16], F32, 143 * K)
        iota = at("iota", [P, L], F32, 147 * K)
        angm = at("angm", [P, 2, L], F32, 148 * K)
        s5in = at("s5in", [P, 3, S5T], F32, 125 * K)
        craw = at("craw", [P, 2, S5T, 16], F32, 112 * K)
        ctmp = at("ctmp", [P, 2, S5T, 16], F32, 116 * K)
        s5p = at("s5p", [P, 21, S5T], F32, 120 * K)
        s5i = at("s5i", [P, S5T], I32, 123 * K)
        iotai = at("iotai", [P, L], I32, 124 * K)
        xsq = at("xsq", [P, 2, 4, L], F32, 128 * K)
        W = 176 * K
        dec = [at(f"dec{k}", [P, HALF, ML], F32, W + k * 4608) for k in range(2)]
        xst = at("xst", [P, TPG, L], F32, W + 9216)
        xtok = at("xtok", [P, 2, HPG * 64], F32, W + 12288)
        cbm = at("cbm", [P, ML], F32, W + 15360)
        mask = at("mask", [P, ML], F32, W + 16896)
        mask_in = at("mask_in", [P, ML], F32, W + 18432)
        ident = at("ident", [P, P], F32, W + 19968)
        dtt = at("dtt", [P, 2, HEADS], F32, W + 20480)
        dtw = at("dtw", [P, 7, L], F32, W)
        C = W + 21 * K
        hw = at("hw", [P, 2, L], F32, 189 * K)
        hsum = at("hsum", [P, 2, L], F32, C)
        tsum = at("tsum", [P, 2, L], F32, C + 2048)
        rot3 = at("rot3", [P, 2, L], F32, C + 2048)
        bst = at("bst", [P, L], F32, C + 2048)
        cpad = at("cpad", [P, 2, L + 4], F32, C + 4096)
        parm = at("parm", [P, N_PARM], F32, C + 6208)
        rs = at("rs", [P, L], F32, C + 8832)
        sq = at("sq", [P, 2, L], F32, 185 * K)
        sqacc = at("sqacc", [P, 2, L], F32, 187 * K)
        ones = at("ones", [P, P], F32, C + 9856)
        s5k = at("s5k", [P, 2, S5T], F32, C + 10368)
        dtp = at("dtp", [P, 3], F32, C + 10624)
        scr = nc.dram_tensor("decay_rows", (HEADS, L), F32).ap()

        psum = ctx.enter_context(nc.psum_tensor("psum", [P, 8, 512], F32))
        BU = [psum[:, b, :].rearrange("p (c n) -> p c n", c=2) for b in (4, 6)]
        YS5 = psum[:, 5, 0:L]
        CB, XP = psum[:, 4, 0:ML], [psum[:, 5, 0:ML], psum[:, 6, 0:ML]]
        YY = [psum[:, 7, 0:L], psum[:, 7, L:2 * L], psum[:, 4, 0:L]]
        NS = psum[:, 7, 0:L]
        DTT = psum[:, 5, 0:2 * HEADS].rearrange("p (s h) -> p s h", s=2)

        def sem(name):
            return ctx.enter_context(nc.semaphore(name))

        x_in, w_in, b_in = [[sem(f"{n}{k}") for k in range(4)] for n in ("x_in", "w_in", "b_in")]
        parm_in, s5_in, h_in, out_done, scr_w = map(sem, ("parm_in", "s5_in", "h_in", "out_done", "scr_w"))
        dec_in = [sem("dec_in0"), sem("dec_in1")]
        hi_ready, lo_ready, unit_used, hsum_ready, sum_ready = map(
            sem, ("hi_ready", "lo_ready", "unit_used", "hsum_ready", "sum_ready"))
        dve_step, act_step, pool_step, const_ready = map(sem, ("dve_step", "act_step", "pool_step", "const_ready"))
        s5_square, s5_inv, dtp_in = sem("s5_square"), sem("s5_inv"), sem("dtp_in")
        xsq_used, xw_ready, xwhi_ready, xwlo_ready, u_ready, s5p_ready, hw_ready, hwhi_ready, hwlo_ready = map(
            sem, ("xsq_used", "xw_ready", "xwhi_ready", "xwlo_ready", "u_ready", "s5p_ready", "hw_ready", "hwhi_ready",
                  "hwlo_ready"))
        xsq_ready, sq_ready, sqacc_ready, ns_ready, rs_ready, v_ready, vhi_ready, vlo_ready = map(
            sem, ("xsq_ready", "sq_ready", "sqacc_ready", "ns_ready", "rs_ready", "v_ready", "vhi_ready", "vlo_ready"))
        dt_in, dt_exp, dt_row, dt_T, dt_v = map(sem, ("dt_in", "dt_exp", "dt_row", "dt_T", "dt_v"))
        iota_ready, angm_ready, tap_ready = map(sem, ("iota_ready", "angm_ready", "tap_ready"))
        th_ready, sincos, bu_ready, ang_ready, tab_ready, x5_ready, y5_ready, cz_ready, y5_out, y5_gelu, y5_hi, y5_lo = map(
            sem, ("th_ready", "sincos", "bu_ready", "ang_ready", "tab_ready", "x5_ready", "y5_ready", "cz_ready",
                  "y5_out", "y5_gelu", "y5_hi", "y5_lo"))
        z_done, conv_done, xbc_done, staged, cb_ready, xp_ready, scan_ready, exp_ready, m_ready, y_ready = map(
            sem, ("z_done", "conv_done", "xbc_done", "staged", "cb_ready", "xp_ready", "scan_ready", "exp_ready",
                  "m_ready", "y_ready"))
        yz_ready, ysq_ready, yns_ready, yrs_ready, yv_ready, yhi_ready, ylo_ready = map(
            sem, ("yz_ready", "ysq_ready", "yns_ready", "yrs_ready", "yv_ready", "yhi_ready", "ylo_ready"))
        ga_sig, gb_sig, glu_sig, m_sum, m_hi, m_lo, conv2_done, silu2_done, f_sum, f_hi, f_lo = map(
            sem, ("ga_sig", "gb_sig", "glu_sig", "m_sum", "m_hi", "m_lo", "conv2_done", "silu2_done", "f_sum",
                  "f_hi", "f_lo"))

        block = ctx.enter_context(nc.Block())

        def col(name, n):
            return parm[:, ds(n + PARM[name], 1)]

        def sums(g, half):
            b = 2 * (g % 2)
            return psum[:, b:b + 2, half * L:half * L + L]

        @block.sync
        def _(sp):
            for c in range(4):
                sp.dma_start(xin[:, 4 * c:4 * c + 4, :], a["x"][:, 4 * c:4 * c + 4, :]).then_inc(x_in[c], 16)
                if c == 0:
                    sp.dma_start(parm[:, :], a["parm"]).then_inc(parm_in, 16)
            for n in range(RING):
                sp.dma_start(raw[:, n, :], a["w_dt"][n]).then_inc(w_in[n], 16)
            sp.dma_start(dtp[0:HEADS, 0:2], a["dtp"]).then_inc(dtp_in, 16)
            sp.dma_start(s5in[:, :, :], a["s5_lam"]).then_inc(s5_in, 16)
            sp.dma_start(craw[:, :, :, :], a["s5_c"]).then_inc(s5_in, 16)
            for name in list(PHASES)[1:]:
                groups, quads, per = PHASES[name]
                with sp.Fori(0, groups // per) as i:
                    for j in range(per * quads):
                        n = UNIT0[name] + j
                        sp.wait_ge(lo_ready, i * (per * quads) + (n - RING + 1))
                        sp.dma_start(raw[:, n % RING, :],
                                     a["w_" + name][ds(i * (per * quads) + j, 1), :, :]
                                     .rearrange("o p n -> (o p) n")).then_inc(w_in[n % RING], 16)
            for c in range(4):
                sp.wait_ge(v_ready, 4 + c + 1)
                sp.dma_start(out[:, 4 * c:4 * c + 4, :], vn[:, 4 * c:4 * c + 4, :]).then_inc(out_done, 16)
            sp.wait_ge(out_done, 64)

        @block.gpsimd
        def _(pool):
            step = Tally(pool, pool_step)
            G = nc.gpsimd
            nc.gpsimd.memset(ones[:, :], 1.0).then_inc(const_ready, 1)
            step.done(nc.gpsimd.memset(bz[:, :, :, :], 0.0))

            def load_b(blk, r):
                for g in range(2):
                    pool.dma_start(bz[32 * r + 16 * g:32 * r + 16 * g + 16, r, :, 64 * g:64 * g + 64],
                                   a["s5_b"][ds(blk * 8 + (2 * r + g), 1), :, :, :]
                                   .rearrange("o c k n -> (o c) k n")).then_inc(b_in[r], 16)

            def load_decay(g, half):
                rows = scr[ds(g * HPG + half * HALF, HALF), :]
                for lo, off in ((0, 0), (P, L)):
                    pool.dma_start(dec[half][:, :, off:off + L - lo],
                                   rows[:, lo:L].rearrange("(o h) n -> o h n", o=1).to_broadcast([P, HALF, L - lo])
                                   ).then_inc(dec_in[half], 16)

            for r in range(4):
                load_b(0, r)
            nc.gpsimd.memset(cz[:, :, :, :], 0.0).then_inc(const_ready, 1)
            nc.gpsimd.memset(cpad[:, :, :], 0.0).then_inc(const_ready, 1)
            nc.gpsimd.iota(iotai[:, :], pattern=[[1, L]], base=0, channel_multiplier=0).then_inc(const_ready, 1)
            step.done(nc.gpsimd.memset(ident[:, :], 0.0))
            nc.gpsimd.affine_select(out=ident[:, :], in_=ident[:, :], compare_op=ALU.not_equal, fill=1.0, base=0,
                                    pattern=[[-1, P]], channel_multiplier=1).then_inc(const_ready, 1)
            for m, keep in ((mask, ALU.is_gt), (mask_in, ALU.is_ge)):
                step.done(nc.gpsimd.memset(m[:, :], 1.0))
                for off, width in ((0, L), (L, P)):
                    nc.gpsimd.affine_select(out=m[:, off:off + width], in_=m[:, off:off + width], compare_op=keep,
                                            fill=0.0, base=0, pattern=[[1, width]],
                                            channel_multiplier=-1).then_inc(const_ready, 1)
            def both(to, x, c, y, op0, op1):
                step.done(G.tensor_scalar(s5p[:, 20, :], x, c, None, op0))
                step.done(G.tensor_tensor(to, s5p[:, 20, :], y, op1))

            def horner(to, x, coefs):
                step.done(G.tensor_scalar(to, x, coefs[0], None, ALU.mult))
                for c in coefs[1:]:
                    both(to, to, c, x, ALU.add, ALU.mult)

            def mul(to, x, y, op=ALU.mult):
                step.done(G.tensor_tensor(to, x, y, op))

            s = [s5p[:, k, :] for k in range(20)]
            lam_im, angle, modulus = s5in[:, 1, :], s5k[:, 0, :], s5k[:, 1, :]
            pool.wait_ge(s5_in, 32)
            pool.wait_ge(const_ready, 9)
            G.tensor_copy(iota[:, :], iotai[:, :]).then_inc(iota_ready, 1)
            step.done(G.tensor_scalar(s[0], s5in[:, 0, :], EIG_MAX, None, ALU.min))
            mul(s[14], s[0], s[0])
            mul(s[15], lam_im, lam_im)
            G.tensor_tensor(s[14], s[14], s[15], ALU.add).then_inc(s5_square, 1)
            step.done(G.tensor_scalar(s[1], s5in[:, 2, :], -87.0, 88.0, ALU.max, ALU.min))
            step.done(G.tensor_scalar(s[2], s[1], LOG2E, MAGIC, ALU.mult, ALU.add))
            step.done(G.tensor_scalar(s[2], s[2], MAGIC, None, ALU.subtract))
            both(s[1], s[2], -LN2_HI, s[1], ALU.mult, ALU.add)
            both(s[1], s[2], -LN2_LO, s[1], ALU.mult, ALU.add)
            horner(s[3], s[1], [1.0 / math.factorial(k) for k in range(7, 0, -1)])
            step.done(G.tensor_scalar(s5i[:, :], s[2], 127.0, 8388608.0, ALU.add, ALU.mult))
            both(s[4], s[3], 1.0, s5i[:, :].bitcast(F32), ALU.add, ALU.mult)
            mul(s[6], lam_im, s[4])
            step.done(G.tensor_scalar(s[6], s[6], 1.0 / (2 * math.pi), None, ALU.mult))
            step.done(G.tensor_scalar(s[7], s[6], MAGIC, None, ALU.add))
            step.done(G.tensor_scalar(s[7], s[7], MAGIC, None, ALU.subtract))
            mul(s[6], s[6], s[7], ALU.subtract)
            G.tensor_scalar(angle, s[6], 0.5, -0.5, ALU.min, ALU.max).then_inc(th_ready, 1)
            mul(s[5], s[0], s[4])
            step.done(G.tensor_scalar(s[5], s[5], -88.0, 1.0 / 256, ALU.max, ALU.mult))
            horner(s[8], s[5], [1.0 / math.factorial(k) for k in range(6, 0, -1)])
            for _ in range(8):
                both(s[8], s[8], 2.0, s[8], ALU.add, ALU.mult)
            step.done(G.tensor_scalar(modulus, s[8], 1.0, None, ALU.add))
            pool.wait_ge(sincos, 2)
            both(s[11], s[10], 2.0, s[10], ALU.mult, ALU.mult)
            mul(s[12], modulus, s[11])
            mul(s[12], s[8], s[12], ALU.subtract)
            mul(s[13], modulus, s[9])
            pool.wait_ge(s5_inv, 1)
            mul(s[16], s[12], s[0])
            mul(s[17], s[13], lam_im)
            mul(s[16], s[16], s[17], ALU.add)
            mul(s[16], s[16], s[15])
            mul(s[18], s[13], s[0])
            mul(s[19], s[12], lam_im)
            mul(s[18], s[18], s[19], ALU.subtract)
            mul(s[18], s[18], s[15])
            def wide(k):
                return s5p[:, k:k + 1, :].rearrange("p o j -> p j o").to_broadcast([P, S5T, 16])
            cr, ci, t0, t1 = craw[:, 0], craw[:, 1], ctmp[:, 0], ctmp[:, 1]
            mul(t0, cr, wide(16))
            mul(t1, ci, wide(18))
            mul(cfold[:, 0], t0, t1, ALU.subtract)
            mul(t0, cr, wide(18))
            mul(t1, ci, wide(16))
            step.done(G.tensor_scalar(t0, t0, -1.0, None, ALU.mult))
            G.tensor_tensor(cfold[:, 1], t0, t1, ALU.subtract).then_inc(s5p_ready, 1)
            pool.wait_ge(dt_row, 1)
            pool.dma_start(scr[:, :], dtw[0:HEADS, 5, :]).then_inc(scr_w, 16)
            with pool.Fori(0, 7) as i:
                for r in range(4):
                    pool.wait_ge(bu_ready, i * 4 + (r + 1))
                    load_b(i + 1, r)
            pool.wait_ge(scr_w, 16)
            pool.wait_ge(dt_v, 1)
            for half in range(2):
                load_decay(0, half)
            with pool.Fori(0, GROUPS - 1) as i:
                for half in range(2):
                    pool.wait_ge(y_ready, i * 2 + (half + 1))
                    load_decay(i + 1, half)
            pool.wait_ge(unit_used, UNIT0["out"])
            pool.dma_start(h[:, :, :], a["x"]).then_inc(h_in, 16)
            for n in range(2):
                pool.wait_ge(ns_ready, n + 1)
                pool.wait_ge(sum_ready, GROUP0["out" if n == 0 else "down"])
                nc.gpsimd.memset(sqacc[:, :, :], 0.0).then_inc(sqacc_ready, 1)
                with pool.Fori(0, 8) as i:
                    pool.wait_ge(sqacc_ready, i + (9 * n + 1))
                    pool.wait_ge(sq_ready, i + (8 * n + 1))
                    nc.gpsimd.tensor_tensor(sqacc[:, :, :], sqacc[:, :, :], sq[:, :, :],
                                            ALU.add).then_inc(sqacc_ready, 1)

        @block.scalar
        def _(act):
            step = Tally(act, act_step)
            fn = nc.scalar.activation

            def split_hi(n, ahead=0):
                s = n % RING
                act.wait_ge(w_in[s], ahead * (16 // RING) + 16 * (n // RING + 1))
                if n >= RING:
                    act.wait_ge(unit_used, ahead + (n - RING + 1))
                fn(whi[:, s, :], raw[:, s, :], ACTF.Copy).then_inc(hi_ready, 1)

            def take_hsum(g, end, gi=0, ui=0):
                act.wait_ge(unit_used, ui + end)
                if g:
                    act.wait_ge(sum_ready, gi + g)
                tiles = slice(0, 2 if g else 1)
                fn(hsum[:, tiles, :], sums(g, 1)[:, tiles, :], ACTF.Copy).then_inc(hsum_ready, 1)

            def root(count, to):
                step.done(fn(rs[:, :], NS, ACTF.Ln, bias=EPS, scale=1.0 / count))
                fn(rs[:, :], rs[:, :], ACTF.Exp, scale=-0.5).then_inc(to, 1)

            def phase(name):
                groups, quads, per = PHASES[name]
                return groups // per, per, quads, UNIT0[name], GROUP0[name]

            def squares(c):
                act.wait_ge(x_in[c], 16)
                if c >= 2:
                    act.wait_ge(xsq_used, c - 1)
                fn(xsq[:, c % 2], xin[:, 4 * c:4 * c + 4, :], ACTF.Square).then_inc(xsq_ready, 1)

            def weighed_hi(c):
                act.wait_ge(xw_ready, c + 1)
                fn(nw[:, 4 * c:4 * c + 4, 0:L], xin[:, 4 * c:4 * c + 4, :], ACTF.Copy).then_inc(xwhi_ready, 1)

            squares(0)
            squares(1)
            weighed_hi(0)
            squares(2)
            weighed_hi(1)
            squares(3)
            weighed_hi(2)
            split_hi(0)
            weighed_hi(3)
            for n in range(1, RING):
                split_hi(n)
            act.wait_ge(ns_ready, 1)
            root(D_MODEL, rs_ready)

            for j in range(4):
                split_hi(RING + j)
            take_hsum(0, 4)
            act.wait_ge(dtp_in, 16)
            fn(dtp[0:HEADS, 2:3], dtp[0:HEADS, 1:2], ACTF.Exp).then_inc(dt_exp, 1)
            act.wait_ge(dt_in, 1)
            fn(dtw[0:HEADS, 2, :], dtw[0:HEADS, 1, :], ACTF.Exp).then_inc(dt_exp, 1)
            act.wait_ge(th_ready, 1)
            fn(s5p[:, 9, :], s5k[:, 0, :], ACTF.Sin, scale=TWO_PI).then_inc(sincos, 1)
            fn(s5p[:, 10, :], s5k[:, 0, :], ACTF.Sin, scale=TWO_PI / 2).then_inc(sincos, 1)

            turns, per, quads, u0, g0 = phase("u")
            with act.Fori(0, turns) as i:
                for r in range(per):
                    for j in range(quads):
                        split_hi(u0 + r * quads + j + RING, i * (per * quads))
                        if j == 1:
                            act.wait_ge(v_ready, i * 2 + (r + 1))
                            act.nop(nofuse=True)
                            q = ds(i * 8 + 4 * r, 4)
                            fn(act16[:, q, 0:L], xin[:, q, :], ACTF.Copy).then_inc(vhi_ready, 1)
                    take_hsum(g0 + r, u0 + (r + 1) * quads, i * per, i * (per * quads))

            def angles(tile):
                f = s5k[:, 0, ds(tile, 1)]
                step.begun(fn(ang[:, 0, :], iota[:, :], ACTF.Identity, scale=f))
                step.done(fn(ang[:, 1, :], iota[:, :], ACTF.Identity, scale=f, bias=0.25))
                fn(angm[:, :, :], ang[:, :, :], ACTF.Identity, bias=MAGIC).then_inc(angm_ready, 1)

            def sines(k, count):
                act.wait_ge(ang_ready, count)
                fn(tab[k][:, :, :], ang[:, :, :], ACTF.Sin, scale=-TWO_PI).then_inc(tab_ready, 1)

            def group_hsum(name, i, r):
                _, per, quads, u0, g0 = phase(name)
                take_hsum(g0 + r, u0 + (r + 1) * quads, i * per, i * (per * quads))

            def group_tap(name, i, r):
                _, per, quads, u0, g0 = phase(name)
                if name == "zx" and r % 2 == 0:
                    return
                act.wait_ge(sum_ready, i * per + (g0 + r + 1))
                act.nop(nofuse=True)
                for t in range(2):
                    if name == "zx":
                        to, q = zx[:, ds(i * 4 + (r - 1 + t), 1), 1, :], i * 4 + (r - 1 + t)
                    else:
                        to, q = bc[:, ds(i * 4 + r, 1), t, :], i * 8 + (24 + 2 * r + t)
                    ins = fn(to.rearrange("p o n -> p (o n)"), cpad[:, t, 3:3 + L], ACTF.Identity,
                             scale=col("conv_a_w", q * 4 + 3), bias=col("conv_a_b", q))
                ins.then_inc(tap_ready, 1)

            def group_silu(name, i, r):
                _, per, quads, u0, g0 = phase(name)
                if name == "zx" and r % 2 == 0:
                    act.wait_ge(sum_ready, i * per + (g0 + r + 1))
                    to = zx[:, ds(i * 4 + r, 2), 0, :]
                    fn(to, to, ACTF.Silu).then_inc(z_done, 1)
                elif name == "zx":
                    act.wait_ge(conv_done, i * 2 + (r // 2 + 1))
                    act.nop(nofuse=True)
                    to = zx[:, ds(i * 4 + (r - 1), 2), 1, :]
                    fn(to, to, ACTF.Silu).then_inc(xbc_done, 1)
                else:
                    act.wait_ge(conv_done, i * per + (12 + r + 1))
                    to = bc[:, ds(i * 4 + r, 1), :, :].rearrange("p o c n -> p (o c) n")
                    fn(to, to, ACTF.Silu).then_inc(xbc_done, 1)

            def mixer_turn(name, i, blk, prev):
                _, per, quads, u0, g0 = phase(name)
                for r in range(per):
                    def hi(j):
                        split_hi(u0 + r * quads + j + RING, i * (per * quads))
                    before = (name, i, r - 1) if r else prev
                    last = name == "bc" and i == 1 and r == per - 1
                    if before:
                        group_hsum(*before)
                    hi(0)
                    if before:
                        group_tap(*before)
                    if not last:
                        act.wait_ge(tab_ready, blk * 4 + (r + 1))
                        angles(blk * 4 + (r + 1))
                    hi(1)
                    if before:
                        group_silu(*before)
                    hi(2)
                    hi(3)
                    if not last:
                        if before:
                            act.wait_ge(x5_ready, blk * 4 + r)
                        sines((r + 1) % 2, blk * 4 + (r + 2))

            act.wait_ge(iota_ready, 1)
            act.wait_ge(th_ready, 1)
            angles(0)
            sines(0, 1)
            mixer_turn("zx", 0, 0, None)
            with act.Fori(1, 6) as i:
                step.enter(i, 8, 1)
                mixer_turn("zx", i, i, ("zx", i - 1, 3))
                step.leave(6)
            mixer_turn("bc", 0, 6, ("zx", 5, 3))
            mixer_turn("bc", 1, 7, ("bc", 0, 3))
            def group_root(g):
                act.wait_ge(yns_ready, g + 1)
                root(TPG * P, yrs_ready)

            def group_hi(g):
                act.wait_ge(yv_ready, g + 1)
                fn(y_hl[:, ds(g * TPG, TPG), 0:L], zx[:, ds(g * TPG, TPG), 1, :], ACTF.Copy).then_inc(yhi_ready, 1)

            def gate_turn(i, prev):
                _, per, quads, u0, g0 = phase("gate")

                def hi(j):
                    split_hi(u0 + j + RING, i * 8)

                def decay(half):
                    act.wait_ge(scan_ready, i * 2 + (half + 1))
                    fn(dec[half][:, :, :], dec[half][:, :, :], ACTF.Exp).then_inc(exp_ready, 1)

                if prev is None:
                    group_hsum("bc", 1, 3)
                    act.wait_ge(x5_ready, 32)
                    act.wait_ge(y5_ready, 31)
                    act.wait_ge(xbc_done, 16)
                fn(bst[:, :], bc[:, ds(i, 1), 0, :].rearrange("p o n -> p (o n)"), ACTF.Copy).then_inc(staged, 1)
                fn(xst[:, :, :], zx[:, ds(i * TPG, TPG), 1, :], ACTF.Copy).then_inc(staged, 1)
                hi(0)
                if prev is not None:
                    group_root(prev)
                else:
                    group_tap("bc", 1, 3)
                hi(1)
                if prev is None:
                    group_silu("bc", 1, 3)
                    act.wait_ge(xbc_done, 20)
                    act.wait_ge(z_done, 12)
                decay(0)
                hi(2)
                hi(3)
                decay(1)
                take_hsum(g0, u0 + 4, i * 2, i * 8)
                hi(4)
                if prev is not None:
                    group_hi(prev)
                hi(5)
                hi(6)
                hi(7)
                act.wait_ge(yz_ready, i + 1)
                fn(zx[:, ds(i * TPG, TPG), 0, :], zx[:, ds(i * TPG, TPG), 1, :], ACTF.Square).then_inc(ysq_ready, 1)
                take_hsum(g0 + 1, u0 + 8, i * 2, i * 8)

            gate_turn(0, None)
            with act.Fori(1, GROUPS) as i:
                step.enter(i, 1, 1)
                gate_turn(i, i - 1)
                step.leave(GROUPS)
            group_root(GROUPS - 1)
            group_hi(GROUPS - 1)

            act.wait_ge(y5_out, 8)
            fn(ub[:, :, :], ub[:, :, :], ACTF.Gelu_apprx_tanh).then_inc(y5_gelu, 1)
            act.wait_ge(y5_gelu, 1)
            act.wait_ge(ylo_ready, 8)
            fn(yb_hl[:, :, 0:L], ub[:, :, :], ACTF.Copy).then_inc(y5_hi, 1)
            act.wait_ge(sum_ready, GROUP0["proj"])

            turns, per, quads, u0, g0 = phase("proj")
            with act.Fori(0, turns) as i:
                for r in range(per):
                    to = gates[:, ds(i * 4 + 2 * r, 2), :]
                    fn(to, to, ACTF.Sigmoid).then_inc(ga_sig, 1)
                    for j in range(quads):
                        split_hi(u0 + r * quads + j + RING, i * (per * quads))
                    take_hsum(g0 + r, u0 + (r + 1) * quads, i * per, i * (per * quads))

            def glu_sigmoid(g):
                act.wait_ge(sum_ready, g + (GROUP0["glu"] + 1))
                fn(tsum[:, 1, :], tsum[:, 1, :], ACTF.Sigmoid).then_inc(glu_sig, 1)

            def merged_hi(g):
                act.wait_ge(m_sum, g + 1)
                fn(act16[:, ds(g, 1), 0:L], gates[:, ds(g, 1), :], ACTF.Copy).then_inc(m_hi, 1)

            def glu_turn(i, r, prev):
                _, per, quads, u0, g0 = phase("glu")
                to = gates[:, ds(i * 2 + (16 + r), 1), :]
                fn(to, to, ACTF.Sigmoid).then_inc(gb_sig, 1)
                split_hi(u0 + r * 2 + RING, i * 4)
                if prev is not None:
                    glu_sigmoid(prev)
                split_hi(u0 + r * 2 + 1 + RING, i * 4)
                if prev is not None:
                    merged_hi(prev)
                take_hsum(g0 + r, u0 + (r + 1) * 2, i * 2, i * 4)

            glu_turn(0, 0, None)
            glu_turn(0, 1, 0)
            with act.Fori(1, 8) as i:
                glu_turn(i, 0, i * 2 - 1)
                glu_turn(i, 1, i * 2)
            glu_sigmoid(15)
            merged_hi(15)

            def weighed_h_hi(g):
                act.wait_ge(hw_ready, g + 1)
                act.nop(nofuse=True)
                fn(nw[:, ds(g * 2, 2), 0:L], hw[:, :, :], ACTF.Copy).then_inc(hwhi_ready, 1)

            def residual_phase(name, n, i, r, prev=None, last=False):
                groups, quads, per = PHASES[name]
                u0, g0 = UNIT0[name], GROUP0[name]
                for j in range(quads):
                    if not (last and r == per - 1 and j >= quads - RING):
                        split_hi(u0 + r * quads + j + RING, i * (per * quads))
                    if prev is not None and j == 1:
                        weighed_h_hi(prev)
                take_hsum(g0 + r, u0 + (r + 1) * quads, i * per, i * (per * quads))
                act.wait_ge(sum_ready, i * per + (g0 + r + 1))
                act.wait_ge(sqacc_ready, i * per + (9 * n + r + 1))
                fn(sq[:, :, :], h[:, ds(i * (2 * per) + 2 * r, 2), :], ACTF.Square).then_inc(sq_ready, 1)

            residual_phase("out", 0, 0, 0)
            residual_phase("out", 0, 0, 1, 0)
            with act.Fori(1, 4) as i:
                residual_phase("out", 0, i, 0, i * 2 - 1)
                residual_phase("out", 0, i, 1, i * 2)
            weighed_h_hi(7)

            def ff_silu(g):
                act.wait_ge(conv2_done, g + 1)
                fn(tsum[:, 0, :], tsum[:, 0, :], ACTF.Silu).then_inc(silu2_done, 1)

            def ff_hi(g, skip=0):
                act.wait_ge(f_sum, g + 1)
                fn(ff[:, ds(g + skip, 1), 0:L], tsum[:, 0:1, :], ACTF.Copy).then_inc(f_hi, 1)

            def up_turn(i, r, prev, skip=0):
                _, per, quads, u0, g0 = phase("up")
                for j in range(4):
                    split_hi(u0 + r * 4 + j + RING, i * 8)
                    if prev is not None and j == 0:
                        ff_silu(prev)
                    if prev is not None and j == 2:
                        ff_hi(prev, skip)
                    if prev is None and j == 2:
                        act.wait_ge(ns_ready, 2)
                        root(D_MODEL, rs_ready)
                take_hsum(g0 + r, u0 + (r + 1) * 4, i * 2, i * 8)

            up_turn(0, 0, None)
            up_turn(0, 1, 0)
            with act.Fori(1, 8) as i:
                up_turn(i, 0, i * 2 - 1)
                up_turn(i, 1, i * 2)
            up_turn(8, 0, 15)
            up_turn(8, 1, 16, KT)
            with act.Fori(9, 22) as i:
                up_turn(i, 0, i * 2 - 1, KT)
                up_turn(i, 1, i * 2, KT)
            ff_silu(43)
            ff_hi(43, KT)

            for i in range(2):
                for r in range(4):
                    residual_phase("down", 1, i, r, last=i == 1)
            act.wait_ge(ns_ready, 3)
            root(D_MODEL, rs_ready)

        @block.vector
        def _(dve):
            step = Tally(dve, dve_step)
            V = nc.vector

            def split_lo(n, ahead=0):
                s = n % RING
                dve.wait_ge(hi_ready, ahead + (n + 1))
                V.tensor_tensor(wlo[:, s, :], raw[:, s, :], whi[:, s, :], ALU.subtract).then_inc(lo_ready, 1)

            def add_halves(to, g, gi=0):
                dve.wait_ge(hsum_ready, gi + (g + 1))
                tiles = slice(0, 2 if g else 1)
                V.tensor_tensor(to, sums(g, 0)[:, tiles, :], hsum[:, tiles, :], ALU.add).then_inc(sum_ready, 1)

            def wide_rs(n):
                return rs[:, :].rearrange("p (o n) -> p o n", o=1).to_broadcast([P, n, L])

            def horner(to, x, coefs):
                step.done(V.tensor_scalar(to, x, coefs[0], None, ALU.mult))
                for c in coefs[1:]:
                    step.done(V.scalar_tensor_tensor(to, to, c, x, ALU.add, ALU.mult))

            def mul(to, x, y, op=ALU.mult):
                step.done(V.tensor_tensor(to, x, y, op))

            def weigh(c):
                dve.wait_ge(xsq_ready, c + 1)
                for k in range(4 * c, 4 * c + 4):
                    ins = V.tensor_scalar(xin[:, k, :], xin[:, k, :], col("norm_mix", k), None, ALU.mult)
                ins.then_inc(xw_ready, 1)

            def weighed_lo(c):
                dve.wait_ge(xwhi_ready, c + 1)
                k = slice(4 * c, 4 * c + 4)
                V.tensor_tensor(nw[:, k, L:2 * L], xin[:, k, :], nw[:, k, 0:L], ALU.subtract).then_inc(xwlo_ready, 1)

            dve.wait_ge(parm_in, 16)
            weigh(0)
            weigh(1)
            weighed_lo(0)
            weigh(2)
            weighed_lo(1)
            weigh(3)
            weighed_lo(2)
            split_lo(0)
            weighed_lo(3)
            for n in range(1, RING):
                split_lo(n)

            for j in range(4):
                split_lo(RING + j)
            add_halves(tsum[:, 0:1, :], 0)
            dve.wait_ge(sum_ready, 1)
            dve.wait_ge(rs_ready, 1)
            mul(tsum[:, 0, :], tsum[:, 0, :], rs[:, :])
            dve.wait_ge(dtp_in, 16)
            d = [dtw[0:HEADS, k, :] for k in range(7)]
            step.done(V.tensor_scalar(d[0], tsum[0:HEADS, 0, :], dtp[0:HEADS, 0:1], None, ALU.add))
            V.scalar_tensor_tensor(d[1], d[0], -1.0, d[0], ALU.mult, ALU.min).then_inc(dt_in, 1)
            dve.wait_ge(dt_exp, 2)
            step.done(V.tensor_scalar(d[3], d[2], 2.0, None, ALU.add))
            step.done(V.reciprocal(d[3], d[3]))
            mul(d[3], d[3], d[2])
            mul(d[4], d[3], d[3])
            horner(d[5], d[4], [1.0 / k for k in (13, 11, 9, 7, 5, 3)])
            step.done(V.scalar_tensor_tensor(d[5], d[5], 1.0, d[3], ALU.add, ALU.mult))
            step.done(V.tensor_scalar(d[0], d[0], 0.0, None, ALU.max))
            step.done(V.scalar_tensor_tensor(d[6], d[5], 2.0, d[0], ALU.mult, ALU.add))
            V.tensor_scalar(d[5], d[6], dtp[0:HEADS, 2:3], -1.0, ALU.mult, ALU.mult).then_inc(dt_row, 1)

            def phase(name):
                groups, quads, per = PHASES[name]
                return groups // per, per, quads, UNIT0[name], GROUP0[name]

            dve.wait_ge(s5_square, 1)
            V.reciprocal(s5p[:, 15, :], s5p[:, 14, :]).then_inc(s5_inv, 1)

            turns, per, quads, u0, g0 = phase("u")
            with dve.Fori(0, turns) as i:
                step.enter(i, 0)
                for r in range(per):
                    x = xin[:, ds(i * 8 + 4 * r, 4), :]
                    for j in range(quads):
                        split_lo(u0 + r * quads + j + RING, i * (per * quads))
                        if j == 0:
                            V.tensor_tensor(x, x, wide_rs(4), ALU.mult).then_inc(v_ready, 1)
                        if j == 2:
                            dve.wait_ge(vhi_ready, i * 2 + (r + 1))
                            to = act16[:, ds(i * 8 + 4 * r, 4), :]
                            V.tensor_tensor(to[:, :, L:2 * L], x, to[:, :, 0:L], ALU.subtract).then_inc(vlo_ready, 1)
                    to = ub[:, ds(i * 4 + 2 * r, 2), :]
                    add_halves(to, g0 + r, i * per)
                    dve.wait_ge(sum_ready, i * per + (g0 + r + 1))
                    V.tensor_tensor(to, to, wide_rs(2), ALU.mult).then_inc(u_ready, 1)
                step.leave(turns)
            dve.wait_ge(dt_T, 1)
            V.tensor_copy(dtt[:, :, :], DTT).then_inc(dt_v, 1)

            sin2, cos2 = [[tab[b][:, k:k + 1, :].to_broadcast([P, 2, L]) for b in range(2)] for k in range(2)]

            def s5_fractions(count):
                dve.wait_ge(angm_ready, count)
                V.scalar_tensor_tensor(ang[:, :, :], angm[:, :, :], MAGIC, ang[:, :, :], ALU.subtract,
                                       ALU.subtract).then_inc(ang_ready, 1)

            def s5_turn_back(r, count, first):
                if not first:
                    dve.wait_ge(x5_ready, count - 1)
                dve.wait_ge(tab_ready, count)
                dve.wait_ge(bu_ready, count)
                step.begun(V.tensor_tensor(rot1[:, :, :], BU[r % 2], cos2[r % 2], ALU.mult))
                step.begun(V.tensor_tensor(rot2[:, :, :], BU[r % 2], sin2[r % 2], ALU.mult))

            def s5_inputs(r, count, first):
                step.hold()
                if not (first and r < 2):
                    dve.wait_ge(y5_ready, count - 2)
                step.begun(V.tensor_tensor(st[r % 2][:, 0, :], rot1[:, 0, :], rot2[:, 1, :], ALU.add))
                step.begun(V.tensor_tensor(st[r % 2][:, 1, :], rot1[:, 1, :], rot2[:, 0, :], ALU.subtract))

            def s5_scan(r, tile):
                step.hold()
                m = s5k[:, 1, ds(tile, 1)].to_broadcast([P, L])
                for k in range(2):
                    step.begun(V.tensor_tensor_scan(rot1[:, k, :], m, st[r % 2][:, k, :], 0.0, ALU.mult, ALU.add))

            def s5_turn_on(r):
                step.hold()
                step.begun(V.tensor_tensor(rot2[:, :, :], rot1[:, :, :], cos2[r % 2], ALU.mult))
                step.begun(V.tensor_tensor(rot3[:, :, :], rot1[:, :, :], sin2[r % 2], ALU.mult))

            def s5_states(r):
                step.hold()
                V.tensor_tensor(st[r % 2][:, 0, :], rot2[:, 0, :], rot3[:, 1, :], ALU.subtract)
                V.tensor_tensor(st[r % 2][:, 1, :], rot2[:, 1, :], rot3[:, 0, :], ALU.add).then_inc(x5_ready, 1)

            def conv_pair(to, tile, taps, w, b, ready, tap_done=False):
                for k in range(taps - (2 if tap_done else 1), -1, -1):
                    off = 3 - (taps - 1) + k
                    for t in range(2):
                        src, q = cpad[:, t, off:off + L], tile + t
                        if k == taps - 1:
                            ins = V.tensor_scalar(to[t], src, col(w, q * taps + k), col(b, q), ALU.mult, ALU.add)
                        else:
                            if not (tap_done and k == taps - 2):
                                step.hold(but=1)
                            ins = V.scalar_tensor_tensor(to[t], src, col(w, q * taps + k), to[t], ALU.mult, ALU.add)
                        if k or not t:
                            step.begun(ins)
                ins.then_inc(ready, 1)

            def s5_out(blk):
                dve.wait_ge(y5_ready, blk * 4 + 4)
                to = ub[:, ds(blk, 1), :].rearrange("p o n -> p (o n)")
                V.scalar_tensor_tensor(to, to, col("s5_d", blk), YS5, ALU.mult, ALU.add).then_inc(y5_out, 1)

            def group_sums(name, i, r):
                _, per, quads, u0, g0 = phase(name)
                if name == "zx" and r % 2 == 0:
                    add_halves(zx[:, ds(i * 4 + r, 2), 0, :], g0 + r, i * per)
                else:
                    add_halves(cpad[:, :, 3:3 + L], g0 + r, i * per)

            def group_conv(name, i, r):
                _, per, quads, u0, g0 = phase(name)
                if name == "zx" and r % 2 == 0:
                    return
                if name == "zx":
                    dve.wait_ge(tap_ready, i * 2 + (r // 2 + 1))
                else:
                    dve.wait_ge(tap_ready, i * per + (12 + r + 1))
                if name == "zx":
                    to = [zx[:, ds(i * 4 + (r - 1 + t), 1), 1, :].rearrange("p o n -> p (o n)") for t in range(2)]
                    conv_pair(to, i * 4 + (r - 1), 4, "conv_a_w", "conv_a_b", conv_done, True)
                else:
                    to = [bc[:, ds(i * 4 + r, 1), t, :].rearrange("p o n -> p (o n)") for t in range(2)]
                    conv_pair(to, i * 8 + (24 + 2 * r), 4, "conv_a_w", "conv_a_b", conv_done, True)

            def cpad_free(name, i, r):
                if name == "bc":
                    dve.wait_ge(conv_done, i * 4 + (12 + r + 1))
                elif r % 2:
                    dve.wait_ge(conv_done, i * 2 + (r // 2 + 1))

            def mixer_turn(name, i, blk, prev):
                _, per, quads, u0, g0 = phase(name)
                for r in range(per):
                    def lo(j):
                        split_lo(u0 + r * quads + j + RING, i * (per * quads))
                    before = (name, i, r - 1) if r else prev
                    last = name == "bc" and i == 1 and r == per - 1
                    tile = blk * 4 + r
                    lo(0)
                    if before:
                        group_sums(*before)
                    s5_turn_back(r, blk * 4 + (r + 1), not before)
                    if before:
                        group_conv(*before)
                    s5_inputs(r, blk * 4 + (r + 1), prev is None)
                    lo(1)
                    if before:
                        cpad_free(*before)
                    s5_scan(r, tile)
                    lo(2)
                    if r == 0:
                        if prev:
                            s5_out(blk - 1)
                        for g in range(2):
                            rows = slice(64 * g, 64 * g + 64)
                            ins = V.tensor_copy(cz[rows, :, :, 16 * g:16 * g + 16],
                                                cfold[rows, :, ds(blk * 4, 4), :].rearrange("p c r n -> p r c n"))
                        ins.then_inc(cz_ready, 1)
                    s5_turn_on(r)
                    if not last:
                        s5_fractions(blk * 4 + (r + 2))
                    s5_states(r)
                    lo(3)

            s5_fractions(1)
            dve.wait_ge(s5p_ready, 1)
            mixer_turn("zx", 0, 0, None)
            with dve.Fori(1, 6) as i:
                step.enter(i, 4 * 8 + 2 * 5, 1)
                mixer_turn("zx", i, i, ("zx", i - 1, 3))
                step.leave(6)
            mixer_turn("bc", 0, 6, ("zx", 5, 3))
            mixer_turn("bc", 1, 7, ("bc", 0, 3))
            def group_norm(g):
                dve.wait_ge(yrs_ready, g + 1)
                for k in range(TPG):
                    x = zx[:, ds(g * TPG + k, 1), 1, :].rearrange("p o n -> p (o n)")
                    ins = V.scalar_tensor_tensor(x, x, col("norm_a", g * TPG + k), rs[:, :], ALU.mult, ALU.mult)
                ins.then_inc(yv_ready, 1)

            def group_lo(g):
                q = ds(g * TPG, TPG)
                dve.wait_ge(yhi_ready, g + 1)
                V.tensor_tensor(y_hl[:, q, L:2 * L], zx[:, q, 1, :], y_hl[:, q, 0:L],
                                ALU.subtract).then_inc(ylo_ready, 1)

            def gate_turn(i, prev):
                _, per, quads, u0, g0 = phase("gate")

                def lo(j):
                    split_lo(u0 + j + RING, i * 8)

                def scan(half):
                    dve.wait_ge(dec_in[half], i * 32 + 32)
                    for k in range(HALF):
                        ins = V.tensor_tensor_scan(dec[half][:, k, :], dec[half][:, k, :], mask[:, :], 0.0,
                                                   ALU.add, ALU.mult)
                    ins.then_inc(scan_ready, 1)

                def blocks(half):
                    dve.wait_ge(exp_ready, i * 2 + (half + 1))
                    V.tensor_tensor(dec[half][:, :, :], dec[half][:, :, :],
                                    cbm[:, :].rearrange("p (o n) -> p o n", o=1).to_broadcast([P, HALF, ML]),
                                    ALU.mult).then_inc(m_ready, 1)

                lo(0)
                if prev is None:
                    group_sums("bc", 1, 3)
                    group_conv("bc", 1, 3)
                    s5_out(7)
                scan(0)
                lo(1)
                dve.wait_ge(cb_ready, i + 1)
                V.tensor_tensor(cbm[:, :], CB, mask_in[:, :], ALU.mult)
                dve.wait_ge(xp_ready, i + 1)
                for k in range(2):
                    ins = V.tensor_tensor(
                        xtok[:, k, :].rearrange("p (h n) -> p h n", h=HPG), XP[k].rearrange("p (h n) -> p h n", h=HPG),
                        dtt[:, k, ds(i * HPG, HPG)].rearrange("p (h o) -> p h o", o=1).to_broadcast([P, HPG, 64]),
                        ALU.mult)
                step.done(ins)
                lo(2)
                scan(1)
                if prev is not None:
                    group_norm(prev)
                blocks(0)
                lo(3)
                add_halves(gates[:, ds(i * 4, 2), :], g0, i * 2)
                blocks(1)
                lo(4)
                lo(5)
                if prev is not None:
                    group_lo(prev)
                lo(6)
                if prev is None:
                    dve.wait_ge(xbc_done, 20)
                    dve.wait_ge(z_done, 12)
                dve.wait_ge(y_ready, i * 2 + 2)
                for k in range(TPG):
                    x = zx[:, ds(i * TPG + k, 1), 1, :].rearrange("p o n -> p (o n)")
                    ins = V.scalar_tensor_tensor(x, x, col("d_a", i * TPG + k), YY[k], ALU.mult, ALU.add)
                step.done(ins)
                q = ds(i * TPG, TPG)
                V.tensor_tensor(zx[:, q, 1, :], zx[:, q, 1, :], zx[:, q, 0, :], ALU.mult).then_inc(yz_ready, 1)
                lo(7)
                add_halves(gates[:, ds(i * 4 + 2, 2), :], g0 + 1, i * 2)

            gate_turn(0, None)
            with dve.Fori(1, GROUPS) as i:
                step.enter(i, 2, 1)
                gate_turn(i, i - 1)
                step.leave(GROUPS)
            group_norm(GROUPS - 1)
            group_lo(GROUPS - 1)

            dve.wait_ge(y5_hi, 1)
            V.tensor_tensor(yb_hl[:, :, L:2 * L], ub[:, :, :], yb_hl[:, :, 0:L], ALU.subtract).then_inc(y5_lo, 1)

            turns, per, quads, u0, g0 = phase("proj")
            with dve.Fori(0, turns) as i:
                step.enter(i, 2)
                for r in range(per):
                    for j in range(quads):
                        split_lo(u0 + r * quads + j + RING, i * (per * quads))
                    add_halves(tsum[:, :, :], g0 + r, i * per)
                    dve.wait_ge(sum_ready, i * per + (g0 + r + 1))
                    dve.wait_ge(ga_sig, i * per + (r + 1))
                    to = gates[:, ds(i * 4 + 2 * r, 2), :]
                    mul(to, tsum[:, :, :], to)
                step.leave(turns)

            def merge(g):
                gb, ga = gates[:, ds(g + 16, 1), :], gates[:, ds(g, 1), :]
                dve.wait_ge(glu_sig, g + 1)
                mul(tsum[:, 0, :], tsum[:, 0, :], tsum[:, 1, :])
                mul(tsum[:, 0:1, :], tsum[:, 0:1, :], gb)
                V.tensor_tensor(ga, ga, tsum[:, 0:1, :], ALU.add).then_inc(m_sum, 1)

            def merged_lo(g):
                dve.wait_ge(m_hi, g + 1)
                to = act16[:, ds(g, 1), :]
                V.tensor_tensor(to[:, :, L:2 * L], gates[:, ds(g, 1), :], to[:, :, 0:L], ALU.subtract).then_inc(m_lo, 1)

            def glu_turn(i, r, prev):
                _, per, quads, u0, g0 = phase("glu")
                split_lo(u0 + r * 2 + RING, i * 4)
                if prev is not None:
                    merge(prev)
                split_lo(u0 + r * 2 + 1 + RING, i * 4)
                if prev is not None:
                    merged_lo(prev)
                add_halves(tsum[:, :, :], g0 + r, i * 2)

            glu_turn(0, 0, None)
            glu_turn(0, 1, 0)
            with dve.Fori(1, 8) as i:
                step.enter(i, 4, 1)
                glu_turn(i, 0, i * 2 - 1)
                glu_turn(i, 1, i * 2)
                step.leave(8)
            merge(15)
            merged_lo(15)

            def weigh_h(g):
                if not (isinstance(g, int) and g == 0):
                    dve.wait_ge(hwlo_ready, g)
                dve.wait_ge(sum_ready, g + (GROUP0["out"] + 1))
                for t in range(2):
                    ins = V.tensor_scalar(hw[:, t, :], h[:, ds(g * 2 + t, 1), :].rearrange("p o n -> p (o n)"),
                                          col("norm_ffn", g * 2 + t), None, ALU.mult)
                ins.then_inc(hw_ready, 1)

            def weighed_h_lo(g):
                dve.wait_ge(hwhi_ready, g + 1)
                to = nw[:, ds(g * 2, 2), :]
                V.tensor_tensor(to[:, :, L:2 * L], hw[:, :, :], to[:, :, 0:L], ALU.subtract).then_inc(hwlo_ready, 1)

            def residual_phase(name, i, r, prev=None, last=False):
                groups, quads, per = PHASES[name]
                u0, g0 = UNIT0[name], GROUP0[name]
                for j in range(quads):
                    if not (last and r == per - 1 and j >= quads - RING):
                        split_lo(u0 + r * quads + j + RING, i * (per * quads))
                    if prev is not None and j == 0:
                        weigh_h(prev)
                    if prev is not None and j == 2:
                        weighed_h_lo(prev)
                hg = h[:, ds(i * (2 * per) + 2 * r, 2), :]
                dve.wait_ge(h_in, 16)
                dve.wait_ge(hsum_ready, i * per + (g0 + r + 1))
                mul(hg, hg, hsum[:, :, :], ALU.add)
                V.tensor_tensor(hg, sums(g0 + r, 0), hg, ALU.add).then_inc(sum_ready, 1)

            residual_phase("out", 0, 0)
            residual_phase("out", 0, 1, 0)
            with dve.Fori(1, 4) as i:
                step.enter(i, 2, 1)
                residual_phase("out", i, 0, i * 2 - 1)
                residual_phase("out", i, 1, i * 2)
                step.leave(4)
            weigh_h(7)
            weighed_h_lo(7)

            def ff_product(g):
                dve.wait_ge(silu2_done, g + 1)
                V.tensor_tensor(tsum[:, 0, :], tsum[:, 0, :], tsum[:, 1, :], ALU.mult).then_inc(f_sum, 1)

            def ff_lo(g, skip=0):
                dve.wait_ge(f_hi, g + 1)
                to = ff[:, ds(g + skip, 1), :]
                V.tensor_tensor(to[:, :, L:2 * L], tsum[:, 0:1, :], to[:, :, 0:L], ALU.subtract).then_inc(f_lo, 1)
                dve.wait_ge(f_lo, g + 1)

            def up_turn(i, r, prev, skip=0):
                _, per, quads, u0, g0 = phase("up")
                for j in range(4):
                    split_lo(u0 + r * 4 + j + RING, i * 8)
                    if prev is not None and j == 1:
                        ff_product(prev)
                    if prev is not None and j == 3:
                        ff_lo(prev, skip)
                add_halves(cpad[:, :, 3:3 + L], g0 + r, i * 2)
                dve.wait_ge(sum_ready, i * 2 + (g0 + r + 1))
                dve.wait_ge(rs_ready, 2)
                mul(cpad[:, :, 3:3 + L], cpad[:, :, 3:3 + L], wide_rs(2))
                conv_pair([tsum[:, t, :] for t in range(2)], i * 4 + 2 * r, 3, "conv_f_w", "conv_f_b", conv2_done)

            up_turn(0, 0, None)
            up_turn(0, 1, 0)
            with dve.Fori(1, 8) as i:
                step.enter(i, 12, 1)
                up_turn(i, 0, i * 2 - 1)
                up_turn(i, 1, i * 2)
                step.leave(8)
            up_turn(8, 0, 15)
            up_turn(8, 1, 16, KT)
            with dve.Fori(9, 22) as i:
                step.enter(i, 12, 9)
                up_turn(i, 0, i * 2 - 1, KT)
                up_turn(i, 1, i * 2, KT)
                step.leave(22)
            ff_product(43)
            ff_lo(43, KT)

            for i in range(2):
                for r in range(4):
                    residual_phase("down", i, r, last=i == 1)
            dve.wait_ge(sum_ready, N_ALL)
            dve.wait_ge(rs_ready, 3)
            for k in range(KT):
                ins = V.scalar_tensor_tensor(vn[:, k, :], h[:, k, :], col("norm_final", k), rs[:, :],
                                             ALU.mult, ALU.mult)
                if k % 4 == 3:
                    ins.then_inc(v_ready, 1)

        @block.tensor
        def _(pe):
            mm = nc.tensor.matmul

            def unit(name, r, q, act, i=0):
                groups, quads, per = PHASES[name]
                n, g = UNIT0[name] + r * quads + q, GROUP0[name] + r
                pe.wait_ge(lo_ready, i * (per * quads) + (n + 1))
                if q == 0 and g >= 1:
                    pe.wait_ge(sum_ready, i * per + (g - 1 if g >= 2 else g))
                s, b = n % RING, 2 * (g % 2)
                for k in range(4):
                    row = 4 * q + k
                    x = act[:, row + (KT if name == "down" and row >= KT else 0), :]
                    first, last = q == 0 and k == 0, q == quads - 1 and k == 3
                    for t in range(1 if name == "dt" else 2):
                        cols = slice(k * L + t * P, k * L + t * P + P)
                        mm(psum[:, b + t, :], whi[:, s, cols], x, start=first, stop=False)
                        ins = mm(psum[:, b + t, L:2 * L], wlo[:, s, cols], x[:, 0:L], start=False, stop=last)
                ins.then_inc(unit_used, 1)

            def ones_sum(parts):
                for k, x in enumerate(parts):
                    ins = mm(NS, ones[:, :], x, start=k == 0, stop=k == len(parts) - 1)
                return ins

            pe.wait_ge(const_ready, 1)
            for k in range(KT):
                c = k // 4
                if k % 4 == 0:
                    pe.wait_ge(xsq_ready, c + 1)
                ins = mm(NS, ones[:, :], xsq[:, c % 2, k % 4, :], start=k == 0, stop=k == KT - 1)
                if k % 4 == 3:
                    ins.then_inc(ns_ready if c == 3 else xsq_used, 1)

            for q in range(4):
                pe.wait_ge(xwlo_ready, q + 1)
                unit("dt", 0, q, nw)
            with pe.Fori(0, 2) as i:
                for r in range(2):
                    for q in range(4):
                        unit("u", r, q, nw, i)
            pe.wait_ge(const_ready, 9)
            pe.wait_ge(dt_row, 1)
            for k in range(2):
                ins = nc.tensor.transpose(DTT[:, k, :], dtw[0:HEADS, 6, k * P:k * P + P], ident[0:HEADS, 0:HEADS])
            ins.then_inc(dt_T, 1)
            pe.wait_ge(u_ready, 4)
            pe.wait_ge(vlo_ready, 4)
            def s5_product(r, tile):
                pe.wait_ge(x5_ready, tile + 1)
                for k in range(2):
                    ins = mm(YS5[32 * r:32 * r + 32], cz[:, r, k, :], st[r % 2][:, k, :], start=k == 0, stop=k == 1)
                ins.then_inc(y5_ready, 1)

            def mixer_turn(name, i, blk, prev):
                for r in range(4):
                    pe.wait_ge(b_in[r], blk * 32 + 32)
                    for k in range(2):
                        ins = mm(BU[r % 2][:, k, :], bz[:, r, k, :],
                                 ub[:, ds(blk, 1), :].rearrange("p o n -> p (o n)"), start=True, stop=True)
                    ins.then_inc(bu_ready, 1)
                    for q in range(3):
                        unit(name, r, q, act16, i)
                    if r:
                        if r == 1:
                            pe.wait_ge(cz_ready, blk + 1)
                        s5_product(r - 1, blk * 4 + (r - 1))
                    elif prev is not None:
                        s5_product(3, prev * 4 + 3)
                    unit(name, r, 3, act16, i)

            mixer_turn("zx", 0, 0, None)
            with pe.Fori(1, 6) as i:
                mixer_turn("zx", i, i, i - 1)
            with pe.Fori(0, 2) as i:
                mixer_turn("bc", i, i + 6, i + 5)
            def group_squares(g):
                pe.wait_ge(ysq_ready, g + 1)
                ones_sum([zx[:, ds(g * TPG + t, 1), 0, :].rearrange("p o n -> p (o n)")
                          for t in range(TPG)]).then_inc(yns_ready, 1)

            def gate_turn(i, prev):
                def heads(half):
                    pe.wait_ge(m_ready, i * 2 + (half + 1))
                    for k in range(HALF):
                        hd = half * HALF + k
                        y = YY[hd // 2][64 * (hd % 2):64 * (hd % 2) + 64]
                        x = slice(64 * hd, 64 * hd + 64)
                        mm(y, xtok[:, 0, x], dec[half][:, k, 0:L], start=True, stop=False)
                        ins = mm(y[:, P:L], xtok[:, 1, x], dec[half][:, k, L:ML], start=False, stop=True)
                    ins.then_inc(y_ready, 1)

                unit("gate", 0, 0, act16, i)
                if prev is not None:
                    group_squares(prev)
                else:
                    unit("gate", 0, 1, act16, i)
                    s5_product(3, 31)
                    unit("gate", 0, 2, act16, i)
                    pe.wait_ge(y5_out, 8)
                pe.wait_ge(staged, i * 2 + 2)
                c = bc[:, ds(i, 1), 1, :].rearrange("p o n -> p (o n)")
                mm(CB[:, 0:L], bst[:, 0:P], c, start=True, stop=True)
                mm(CB[:, L:ML], bst[:, P:L], c[:, P:L], start=True, stop=True).then_inc(cb_ready, 1)
                for k in range(2):
                    for t in range(TPG):
                        ins = nc.tensor.transpose(XP[k][:, t * P:t * P + P], xst[:, t, k * P:k * P + P], ident[:, :])
                ins.then_inc(xp_ready, 1)
                for q in range(1 if prev is not None else 3, 4):
                    unit("gate", 0, q, act16, i)
                unit("gate", 1, 0, act16, i)
                heads(0)
                unit("gate", 1, 1, act16, i)
                heads(1)
                unit("gate", 1, 2, act16, i)
                unit("gate", 1, 3, act16, i)

            gate_turn(0, None)
            with pe.Fori(1, GROUPS) as i:
                gate_turn(i, i - 1)
            group_squares(GROUPS - 1)

            def plain_turn(name, i, src, ready=None, need=None):
                groups, quads, per = PHASES[name]
                for r in range(per):
                    for q in range(quads):
                        if ready is not None and r == 0:
                            pe.wait_ge(ready, need(q))
                        unit(name, r, q, src, i)
                        if name == "up" and ready is not None and r == 0 and q == 2:
                            pe.wait_ge(sqacc_ready, 9)
                            ones_sum([sqacc[:, k, :] for k in range(2)]).then_inc(ns_ready, 1)

            for name, src, ready, need in (("proj", y_hl, ylo_ready, lambda q: (4 * q + 3) // TPG + 1),
                                           ("glu", yb_hl, y5_lo, lambda q: 1),
                                           ("out", act16, m_lo, lambda q: 4 * q + 4),
                                           ("up", nw, hwlo_ready, lambda q: 2 * q + 2),
                                           ("down", ff, f_lo, lambda q: 4 * q + 4)):
                groups, quads, per = PHASES[name]
                plain_turn(name, 0, src, ready, need)
                with pe.Fori(1, groups // per) as i:
                    plain_turn(name, i, src)
            pe.wait_ge(sqacc_ready, 18)
            ones_sum([sqacc[:, k, :] for k in range(2)]).then_inc(ns_ready, 1)

    return nc


def _units(w):
    rows, cols = w.shape
    w = w.reshape(rows // 512, 4, P, cols // 256, 256).transpose(3, 0, 2, 1, 4)
    return np.ascontiguousarray(w).reshape(-1, P, UNIT)


def _pairs(x, y, width=P):
    lead = x.shape[:-1]
    x, y = x.reshape(*lead, -1, 1, width), y.reshape(*lead, -1, 1, width)
    return np.concatenate([x, y], axis=-2).reshape(*lead, -1)


def _tiles(v):
    return v.reshape(-1, P).T


def _conv(w):
    return w.reshape(w.shape[0], -1, P).transpose(2, 1, 0).reshape(P, -1)


def kernel(**inputs):
    import concourse.bacc as bacc
    from concourse.bass_utils import run_bass_kernel_spmd

    v = {k: np.asarray(x) for k, x in inputs.items()}
    w_in = v["w_in"][0]
    cut = np.cumsum([0, D_INNER, D_INNER, 1024, 1024, HEADS, D_S5, 2 * D_MODEL])
    z, x, b, c, dt, u, gate = (w_in[:, cut[k]:cut[k + 1]] for k in range(7))
    glu, up = v["w_s5_glu"][0], v["w_up"][0]
    cw, cb, fw, fb = v["conv_a_w"][0], v["conv_a_b"][0], v["conv_ffn_w"][0], v["conv_ffn_b"][0]

    def xbc_order(m):
        return np.concatenate([m[..., :D_INNER], _pairs(m[..., D_INNER:D_INNER + 1024], m[..., D_INNER + 1024:])], axis=-1)

    def halves(m):
        n = m.shape[-1] // 2
        return _pairs(m[..., :n], m[..., n:])

    a = {
        "x": np.ascontiguousarray(v["x"][0].reshape(L, KT, P).transpose(2, 1, 0)),
        "w_dt": _units(w_in[:, cut[4]:cut[4] + 256]), "w_u": _units(u), "w_zx": _units(_pairs(z, x, 256)),
        "w_bc": _units(_pairs(b, c)), "w_gate": _units(gate), "w_proj": _units(v["w_proj_a"][0]),
        "w_glu": _units(halves(glu)), "w_out": _units(v["w_out"][0]), "w_up": _units(halves(up)),
        "w_down": _units(v["w_down"][0]),
        "dtp": np.ascontiguousarray(np.stack([v["dt_bias"][0], v["a_log"][0]], axis=1)),
        "s5_lam": np.ascontiguousarray(np.stack(
            [v["s5_lam_re"][0], v["s5_lam_im"][0],
             np.broadcast_to(v["s5_log_dt"][0][:, None], (64, 64))]).reshape(3, S5T, P).transpose(2, 0, 1)),
        "s5_c": np.ascontiguousarray(np.stack([v["s5_c_re"][0], v["s5_c_im"][0]])
                                     .transpose(0, 1, 3, 2).reshape(2, S5T, P, 16).transpose(2, 0, 1, 3)),
        "s5_b": np.ascontiguousarray(np.stack([v["s5_b_re"][0], v["s5_b_im"][0]]).transpose(1, 3, 0, 2)),
    }
    a["parm"] = np.ascontiguousarray(np.concatenate([
        _tiles(v["norm_mix_w"][0]), _tiles(v["norm_ffn_w"][0]), _tiles(v["norm_final_w"]), _tiles(v["norm_a_w"][0]),
        _tiles(np.repeat(v["d_a"][0], 64)), _conv(xbc_order(cw)), _tiles(xbc_order(cb)), _conv(halves(fw)),
        _tiles(halves(fb)), _tiles(v["s5_d"][0])], axis=1))

    nc = bacc.Bacc("TRN2", target_bir_lowering=False, num_devices=1)
    aps = {k: nc.dram_tensor(f"in_{k}", m.shape, mybir.dt.from_np(m.dtype), kind="ExternalInput").ap()
           for k, m in a.items()}
    out = nc.dram_tensor("out", (P, KT, L), F32, kind="ExternalOutput").ap()
    build_program(nc, aps, out)
    r = run_bass_kernel_spmd(nc, [{f"in_{k}": m for k, m in a.items()}], core_ids=[0])
    y = r.results[0]["out"]
    return np.ascontiguousarray(y.transpose(2, 1, 0)).reshape(1, L, D_MODEL)
```
